# Optimizing a Trainium2 kernel written in Bass

```python
import jax, jax.numpy as jnp
from jax import lax
import numpy as np

D_MODEL = 1024
BATCH = 1
SEQ = 1024
DEPTH = 1

HEAD_DIM = 64
N_HEADS = D_MODEL // HEAD_DIM
N_SB_HEADS = N_HEADS // 2
N_DSA_HEADS = N_HEADS - N_SB_HEADS
SB_WIDTH = N_SB_HEADS * HEAD_DIM
DSA_WIDTH = N_DSA_HEADS * HEAD_DIM
MIX_WIDTH = SB_WIDTH + DSA_WIDTH
KV_LORA = D_MODEL // 4
N_IDX_HEADS = 4
IDX_DIM = 64
TOPK_MAX = 256
Q_BLOCK = 128
D_FF = -(-8 * D_MODEL // (3 * 256)) * 256
RMS_EPS = 1e-6
IN_SIZES = (SB_WIDTH, SB_WIDTH, SB_WIDTH,
            DSA_WIDTH, KV_LORA,
            N_IDX_HEADS * IDX_DIM, IDX_DIM,
            N_IDX_HEADS)
IN_COLS = sum(IN_SIZES)

kernel_name = "hybrid_stickbreak_dsa_adaln_block"

def _rmsnorm(x, gain):
    xf = x.astype(jnp.float32)
    y = xf * lax.rsqrt(jnp.mean(xf * xf, axis=-1, keepdims=True) + RMS_EPS)
    return (y * gain.astype(jnp.float32)).astype(x.dtype)

def _modulate(h, shift, scale):
    return h * (1.0 + scale[:, None, :]) + shift[:, None, :]

def _alibi_slopes(n):
    return 2.0 ** (-8.0 * jnp.arange(1, n + 1, dtype=jnp.float32) / n)

def _stick_breaking_attention(q, k, v):
    B, S, H, dh = q.shape
    scale = dh ** -0.5
    outs = []
    for i in range(S // Q_BLOCK):
        q0, end = i * Q_BLOCK, (i + 1) * Q_BLOCK
        z = jnp.einsum('bthd,bshd->bhts', q[:, q0:end], k[:, :end]).astype(jnp.float32) * scale
        t_pos = q0 + jnp.arange(Q_BLOCK)[:, None]
        s_pos = jnp.arange(end)[None, :]
        causal = s_pos < t_pos
        log_1m_beta = jnp.where(causal, jax.nn.log_sigmoid(-z), 0.0)
        tail = lax.cumsum(log_1m_beta, axis=3, reverse=True) - log_1m_beta
        A = jnp.where(causal, jnp.exp(jax.nn.log_sigmoid(z) + tail), 0.0)
        outs.append(jnp.einsum('bhts,bshd->bthd', A.astype(v.dtype), v[:, :end]))
    return jnp.concatenate(outs, axis=1)

def _dsa_attention(q, k, v, q_idx, k_idx, w_idx, slopes, topk):
    B, S, H, dh = q.shape
    scale = dh ** -0.5
    idx_q_scale = IDX_DIM ** -0.5
    idx_w_scale = N_IDX_HEADS ** -0.5
    b_idx = jnp.arange(B)[:, None, None]
    s_pos = jnp.arange(S)

    def block(i):
        q0 = i * Q_BLOCK
        qb = lax.dynamic_slice_in_dim(q, q0, Q_BLOCK, axis=1)
        qib = lax.dynamic_slice_in_dim(q_idx, q0, Q_BLOCK, axis=1)
        wib = lax.dynamic_slice_in_dim(w_idx, q0, Q_BLOCK, axis=1)
        t_pos = q0 + jnp.arange(Q_BLOCK)
        causal = s_pos[None, :] <= t_pos[:, None]
        idx_logits = jnp.einsum('bthd,bsd->btsh', qib, k_idx).astype(jnp.float32) * idx_q_scale
        score = jnp.einsum('btsh,bth->bts', jax.nn.relu(idx_logits),
                           wib.astype(jnp.float32) * idx_w_scale)
        score = jnp.where(causal[None], score, -jnp.inf)
        _, sel = lax.top_k(score, topk)
        k_sel = k[b_idx, sel]
        v_sel = v[b_idx, sel]
        valid = sel <= t_pos[None, :, None]
        dist = (t_pos[None, :, None] - sel).astype(jnp.float32)
        logits = jnp.einsum('bthd,btkd->bhtk', qb, k_sel).astype(jnp.float32) * scale
        logits = logits - slopes[None, :, None, None] * dist[:, None]
        logits = jnp.where(valid[:, None], logits, -jnp.inf)
        p = jax.nn.softmax(logits, axis=-1)
        return jnp.einsum('bhtk,btkd->bthd', p.astype(v.dtype), v_sel)

    out = lax.map(block, jnp.arange(S // Q_BLOCK))
    return jnp.moveaxis(out, 0, 1).reshape(B, S, H, dh)

def _hybrid_mixer(h, w_in, kv_gain, w_uk, w_uv, sb_out_gain, dsa_out_gain, w_o, slopes, topk):
    B, S, _ = h.shape
    proj = h @ w_in
    sb_q, sb_k, sb_v, dsa_q, kv_lat, idx_q, idx_k, idx_w = jnp.split(
        proj, np.cumsum(IN_SIZES)[:-1], axis=-1)
    sb_heads = lambda t: t.reshape(B, S, N_SB_HEADS, HEAD_DIM)
    o_sb = _stick_breaking_attention(sb_heads(sb_q), sb_heads(sb_k), sb_heads(sb_v))
    kv = _rmsnorm(kv_lat, kv_gain)
    k_d = kv @ w_uk
    v_d = kv @ w_uv
    o_dsa = _dsa_attention(dsa_q.reshape(B, S, N_DSA_HEADS, HEAD_DIM), k_d, v_d,
                           idx_q.reshape(B, S, N_IDX_HEADS, IDX_DIM), idx_k, idx_w,
                           slopes, topk)
    o = jnp.concatenate([_rmsnorm(o_sb.reshape(B, S, SB_WIDTH), sb_out_gain),
                         _rmsnorm(o_dsa.reshape(B, S, DSA_WIDTH), dsa_out_gain)], axis=-1)
    return o @ w_o

def _swiglu(h, w_gate, w_up, w_down):
    return (jax.nn.silu(h @ w_gate) * (h @ w_up)) @ w_down

def setup_inputs(seed: int = 0) -> dict:
    key = jax.random.key(seed)
    ks = jax.random.split(key, 20)
    nrm = lambda k, shape, s: jax.random.normal(k, shape, jnp.float32) * s
    gain = lambda k, shape: 1.0 + nrm(k, shape, 0.02)
    L, D = DEPTH, D_MODEL
    return {
        "x": nrm(ks[0], (BATCH, SEQ, D), 1.0),
        "c": nrm(ks[1], (BATCH, D), 1.0),
        "w_mod": nrm(ks[2], (L, D, 6 * D), 0.5 * D ** -0.5),
        "b_mod": nrm(ks[3], (L, 6 * D), 0.02),
        "norm1_gain": gain(ks[4], (L, D)),
        "norm2_gain": gain(ks[5], (L, D)),
        "w_in": nrm(ks[6], (L, D, IN_COLS), D ** -0.5),
        "kv_gain": gain(ks[7], (L, KV_LORA)),
        "w_uk": nrm(ks[8], (L, KV_LORA, HEAD_DIM), KV_LORA ** -0.5),
        "w_uv": nrm(ks[9], (L, KV_LORA, HEAD_DIM), KV_LORA ** -0.5),
        "sb_out_gain": gain(ks[10], (L, SB_WIDTH)),
        "dsa_out_gain": gain(ks[11], (L, DSA_WIDTH)),
        "w_o": nrm(ks[12], (L, MIX_WIDTH, D), MIX_WIDTH ** -0.5),
        "w_gate": nrm(ks[13], (L, D, D_FF), D ** -0.5),
        "w_up": nrm(ks[14], (L, D, D_FF), D ** -0.5),
        "w_down": nrm(ks[15], (L, D_FF, D), D_FF ** -0.5),
        "w_mod_final": nrm(ks[16], (D, 2 * D), 0.5 * D ** -0.5),
        "b_mod_final": nrm(ks[17], (2 * D,), 0.02),
        "final_gain": gain(ks[18], (D,)),
    }

def reference(x, c, w_mod, b_mod, norm1_gain, norm2_gain, w_in, kv_gain, w_uk, w_uv,
              sb_out_gain, dsa_out_gain, w_o, w_gate, w_up, w_down,
              w_mod_final, b_mod_final, final_gain):
    S = x.shape[1]
    topk = min(TOPK_MAX, S // 4)
    slopes = _alibi_slopes(N_DSA_HEADS)
    c_act = jax.nn.silu(c)
    for l in range(DEPTH):
        mod = c_act @ w_mod[l] + b_mod[l]
        sh1, sc1, g1, sh2, sc2, g2 = jnp.split(mod, 6, axis=-1)
        h = _modulate(_rmsnorm(x, norm1_gain[l]), sh1, sc1)
        x = x + g1[:, None, :] * _hybrid_mixer(h, w_in[l], kv_gain[l], w_uk[l], w_uv[l],
                                               sb_out_gain[l], dsa_out_gain[l], w_o[l],
                                               slopes, topk)
        h = _modulate(_rmsnorm(x, norm2_gain[l]), sh2, sc2)
        x = x + g2[:, None, :] * _swiglu(h, w_gate[l], w_up[l], w_down[l])
    sh_f, sc_f = jnp.split(c_act @ w_mod_final + b_mod_final, 2, axis=-1)
    return _modulate(_rmsnorm(x, final_gain), sh_f, sc_f)


_drawn_inputs = setup_inputs


def setup_inputs(seed=0):
    import zlib

    import numpy as np

    out = dict(_drawn_inputs(seed))
    spreads = {}
    factors = {'norm2_gain': 8.0,
     'kv_gain': 8.0,
     'sb_out_gain': 23.408,
     'dsa_out_gain': 24.233,
     'final_gain': 8.796,
     'b_mod_final': 2.94}
    for name, (base, spread) in spreads.items():
        noise = np.random.default_rng([zlib.crc32(name.encode()), seed]).standard_normal(out[name].shape)
        drawn = base * np.exp(spread * noise) if base else spread * noise
        out[name] = __import__('jax').numpy.asarray(drawn.astype(out[name].dtype))
    for name, factor in factors.items():
        out[name] = (out[name] * factor).astype(out[name].dtype)
    return out
```

```python
from contextlib import ExitStack

import concourse.bass as bass
from concourse import mybir

F32 = mybir.dt.float32
F32R = mybir.dt.float32r
I32 = mybir.dt.int32
ALU = mybir.AluOpType
ACT = mybir.ActivationFunctionType
AX = mybir.AxisListType

P = 128
SEQ = 1024
D = 1024
NT = SEQ // P
KD = D // P
HD = 64
NH = 8
NPAIR = NH // 2
KV = D // 4
NIH = 4
TOPK = 256
FF = 2816
NM = FF // P
EPS = 1e-6
BIG = 1e30
HALF = SEQ // 2
ZCLAMP = 40.0

C_SBQ, C_SBK, C_SBV, C_DQ, C_LAT = 0, 512, 1024, 1536, 2048
C_IQ = C_LAT + KV
C_IK = C_IQ + NIH * HD
IKW = HD + NIH

R_BMOD, R_N1, R_N2, R_KV, R_SBG, R_DG, R_C = 0, 48, 56, 64, 66, 70, 74
NROWS = R_C + KD


def soff(i):
    return P * (i * (i + 1) // 2)


class Kit:

    def __init__(self, nc):
        self.nc, self.used = nc, []

    def sem(self, name):
        self.used.append(self.nc.alloc_semaphore(name=name))
        return self.used[-1]

    def release(self):
        self.nc.clear_and_free_semaphores(self.used)
        self.nc.all_engine_barrier()
        self.used = []

    def sems(self, name, n):
        return [self.sem(f"{name}{i}") for i in range(n)]


def sbuf(nc, ctx, name, shape, dt=F32):
    return ctx.enter_context(nc.sbuf_tensor(name, shape, dt))


def psum(nc, ctx, name, shape, dt=F32):
    return ctx.enter_context(nc.psum_tensor(name, shape, dt))


def phase0(nc, k, g, A):
    with ExitStack() as ctx:
        xt = sbuf(nc, ctx, "xt", [P, NT, D])
        wm = sbuf(nc, ctx, "wm", [P, 2, KD, 512])
        acc = sbuf(nc, ctx, "mod_acc", [P, 4, 512])
        vec = sbuf(nc, ctx, "vec", [P, P])
        junk = sbuf(nc, ctx, "sq_junk", [P, 2, D])
        ss = sbuf(nc, ctx, "ss1", [P, NT])
        ssv = sbuf(nc, ctx, "ssv1", [P, NT])
        rstd = sbuf(nc, ctx, "rstd1", [P, NT])
        mb = sbuf(nc, ctx, "mb1", [P, 16])
        hf = sbuf(nc, ctx, "hfull", [P, 2, HALF])
        ps_t = psum(nc, ctx, "ps_t0", [P, 4, HALF])
        ps_v = psum(nc, ctx, "ps_v0", [P, 512])
        ps_m = psum(nc, ctx, "ps_m0", [P, 512])

        vec_loaded = k.sem("vec_loaded")
        x_loaded = k.sems("x_loaded", NT)
        wm_loaded = k.sems("wm_loaded", 2)
        const0 = k.sem("const_zeroed")
        scales_set = k.sem("scales_set")
        const_ready = k.sem("const_ready")
        vecT = k.sem("vecT_done")
        cols_ready = k.sem("cols_ready")
        csil_ready = k.sem("csil_ready")
        chain = k.sem("mod_chain")
        accd = k.sem("mod_acc_done")
        modm = k.sem("mod_summed")
        mbs = k.sem("mod_biased")
        ab = k.sem("ab1_ready")
        ssd = k.sem("ss1_done")
        ssn = k.sem("ss1_scaled")
        rs = k.sem("rstd1_ready")
        xh = k.sem("xhat_ready")
        tr = k.sem("x_transposed")
        hfs = k.sem("hfull_ready")
        his = k.sem("hhi_ready")
        los = k.sem("hlo_ready")
        rows = [(A["b_mod"], R_BMOD, 48), (A["norm1_gain"], R_N1, KD), (A["norm2_gain"], R_N2, KD),
                (A["kv_gain"], R_KV, 2), (A["sb_out_gain"], R_SBG, 4), (A["dsa_out_gain"], R_DG, 4),
                (A["c"], R_C, KD)]
        w_mod = A["w_mod"][0].rearrange("(t p) n -> p t n", p=P)
        xb = A["x"][0].rearrange("(i p) d -> i p d", p=P)

        with nc.Block() as block:
            @block.sync
            def _(sp):
                for src, r, n in rows:
                    sp.dma_start(vec[r:r + n, :], src.rearrange("a (r p) -> (a r) p", p=P)).then_inc(vec_loaded, 16)
                for i in range(4):
                    sp.dma_start(xt[:, i, :], xb[i]).then_inc(x_loaded[i], 16)
                for j in range(4):
                    if j >= 2:
                        sp.wait_ge(accd, j - 1)
                    sp.dma_start(wm[:, j % 2], w_mod[:, :, 512 * j:512 * j + 512]).then_inc(wm_loaded[j % 2], 16)
                    if j == 1:
                        for i in range(4, NT):
                            sp.dma_start(xt[:, i, :], xb[i]).then_inc(x_loaded[i], 16)

            @block.gpsimd
            def _(pool):
                pool.memset(g.ident[:], 0.0).then_inc(const0, 1)
                pool.memset(g.ones[:], 1.0).then_inc(const0, 1)
                pool.memset(g.tneg_f[:], -1.0).then_inc(const0, 1)
                pool.memset(g.nhalf[:], -0.5).then_inc(const0, 1)
                pool.wait_ge(const0, 4)
                pool.affine_select(out=g.ident[:], in_=g.ident[:], compare_op=ALU.not_equal, fill=1.0,
                                   base=0, pattern=[[-1, P]], channel_multiplier=1).then_inc(const_ready, 1)
                pool.affine_select(out=g.tneg_f[:], in_=g.tneg_f[:], compare_op=ALU.is_ge, fill=0.0,
                                   base=0, pattern=[[-1, P]], channel_multiplier=1).then_inc(const_ready, 1)
                pool.iota(g.dist_i[:], pattern=[[1, SEQ]], base=-(SEQ - P), channel_multiplier=-1).then_inc(const_ready, 1)
                pool.wait_ge(const_ready, 3)
                pool.tensor_copy(g.tneg[:], g.tneg_f[:]).then_inc(const_ready, 1)
                pool.tensor_copy(g.dist[:], g.dist_i[:]).then_inc(const_ready, 1)
                pool.tensor_scalar(g.bigid[:], g.ident[:], BIG, None, ALU.mult).then_inc(const_ready, 1)
                pool.tensor_scalar(g.nneg[:], g.ones[:], -1.0, None, ALU.mult).then_inc(const_ready, 1)
                for j in range(2):
                    pool.wait_ge(ssd, 4 * j + 4)
                    s = slice(4 * j, 4 * j + 4)
                    pool.tensor_scalar(ssv[:, s], ss[:, s], 1.0 / D, EPS, ALU.mult, ALU.add).then_inc(ssn, 1)
                    pool.wait_ge(ssn, j + 1)
                    pool.tensor_tensor(rstd[:, s], ssv[:, s], g.nhalf[:, s], ALU.pow).then_inc(rs, 1)

            @block.scalar
            def _(act):
                act.wait_ge(cols_ready, 1)
                act.activation(g.csil[:], g.cols[:, R_C:R_C + KD], ACT.Silu).then_inc(csil_ready, 1)

                def square(i):
                    act.wait_ge(x_loaded[i], 16)
                    if i >= 2:
                        act.wait_ge(ssd, i - 1)
                    act.activation(junk[:, i % 2], xt[:, i, :], ACT.Square, accum_out=ss[:, i:i + 1]).then_inc(ssd, 1)

                def normalise(i):
                    act.wait_ge(rs, i // 4 + 1)
                    act.activation(xt[:, i, :], xt[:, i, :], ACT.Copy, scale=rstd[:, i:i + 1]).then_inc(xh, 1)

                def modulate(n):
                    t = n % KD
                    act.wait_ge(tr, n + 1)
                    act.wait_ge(ab, 2)
                    if n >= 2:
                        act.wait_ge(los, n - 1)
                    act.activation(hf[:, n % 2], ps_t[:, n % 4], ACT.Identity,
                                   bias=g.b1[:, t:t + 1], scale=g.a1[:, t:t + 1]).then_inc(hfs, 1)

                for i in range(4):
                    square(i)
                for i in range(4):
                    normalise(i)
                for i in range(4, NT):
                    square(i)
                for i in range(4, NT):
                    normalise(i)
                for n in range(2 * KD):
                    modulate(n)

            @block.tensor
            def _(pe):
                pe.wait_ge(const_ready, 2)
                pe.wait_ge(vec_loaded, 16 * len(rows))
                pe.transpose(ps_v[:, 0:NROWS], vec[0:NROWS, :], g.ident[0:NROWS, 0:NROWS]).then_inc(vecT, 1)

                def transposes(n):
                    half, t = n // KD, n % KD
                    pe.wait_ge(xh, 4 * half + 4)
                    if n >= 4:
                        pe.wait_ge(hfs, n - 3)
                    for i in range(4):
                        m = pe.transpose(ps_t[:, n % 4, P * i:P * i + P],
                                         xt[:, 4 * half + i, P * t:P * t + P], g.ident[:])
                    m.then_inc(tr, 1)

                for n in range(4):
                    transposes(n)
                for j in range(4):
                    pe.wait_ge(accd, j + 1)
                    for t in range(4):
                        m = pe.matmul(ps_m[:, 4 * j + t:4 * j + t + 1], acc[:, j, P * t:P * t + P],
                                      g.ones[:, 0:1], start=(j == 0 and t == 0), stop=True,
                                      skip_group_check=True)
                    m.then_inc(modm, 1)
                for n in range(4, 2 * KD):
                    transposes(n)

            @block.vector
            def _(dve):
                for h in range(NH):
                    dve.memset(g.qscale[HD * (h % 2):HD * (h % 2) + HD, 12 + h // 2:13 + h // 2],
                                0.125 * 2.0 ** (h + 1)).then_inc(scales_set, 1)
                    dve.memset(g.nslope[:, h:h + 1], -(2.0 ** -(h + 1))).then_inc(scales_set, 1)
                dve.memset(g.qscale[:, 0:4], 0.125).then_inc(scales_set, 1)
                dve.memset(g.qscale[:, 4:12], 1.0).then_inc(scales_set, 1)
                dve.wait_ge(vecT, 1)
                dve.tensor_copy(g.cols[:, 0:NROWS], ps_v[:, 0:NROWS]).then_inc(cols_ready, 1)
                dve.wait_ge(csil_ready, 1)
                for j in range(4):
                    dve.wait_ge(wm_loaded[j % 2], 16 * (j // 2 + 1))
                    dve.tensor_scalar(acc[:, j], wm[:, j % 2, 0], g.csil[:, 0:1], None, ALU.mult).then_inc(chain, 1)
                    for t in range(1, KD):
                        dve.wait_ge(chain, 7 * j + t)
                        dve.scalar_tensor_tensor(out=acc[:, j], in0=wm[:, j % 2, t], scalar=g.csil[:, t:t + 1],
                                                 in1=acc[:, j], op0=ALU.mult, op1=ALU.add)\
                           .then_inc(chain if t < KD - 1 else accd, 1)
                dve.wait_ge(modm, 4)
                dve.tensor_tensor(mb[:], ps_m[:, 0:16], g.cols[:, 0:16], ALU.add).then_inc(mbs, 1)
                dve.wait_ge(mbs, 1)
                dve.tensor_copy(g.b1[:], mb[:, 0:8]).then_inc(ab, 1)
                dve.scalar_tensor_tensor(out=g.a1[:], in0=mb[:, 8:16], scalar=1.0, in1=g.cols[:, R_N1:R_N1 + 8],
                                         op0=ALU.add, op1=ALU.mult).then_inc(ab, 1)
                for n in range(2 * KD):
                    half, t = n // KD, n % KD
                    s = slice(HALF * half, HALF * half + HALF)
                    dve.wait_ge(hfs, n + 1)
                    dve.tensor_copy(g.hTh[:, t, s], hf[:, n % 2]).then_inc(his, 1)
                    dve.wait_ge(his, n + 1)
                    dve.tensor_tensor(g.hTl[:, t, s], hf[:, n % 2], g.hTh[:, t, s].bitcast(F32),
                                      ALU.subtract).then_inc(los, 1)


def tile_products(pe, ps, wh, wl, xh, xl, halves=2):
    for t in range(KD):
        for w, x in ((wh, xh), (wh, xl), (wl, xh)):
            for f in range(halves):
                s = slice(HALF * f, HALF * f + HALF)
                last = pe.matmul(ps[:, s], w[:, t, :], x[:, t, s], start=(t == 0 and w is wh and x is xh),
                                 stop=(t == KD - 1 and w is wl))
    return last


def phase1(nc, k, g, A, scr):
    with ExitStack() as ctx:
        raw = sbuf(nc, ctx, "win_raw", [P, 2, KD, P])
        wh = sbuf(nc, ctx, "win_hi", [P, 2, KD, P], F32R)
        wl = sbuf(nc, ctx, "win_lo", [P, 2, KD, P], F32R)
        evf = sbuf(nc, ctx, "proj_full", [P, 2, SEQ])
        evh = sbuf(nc, ctx, "proj_hi", [P, 2, SEQ], F32R)
        evl = sbuf(nc, ctx, "proj_lo", [P, 2, SEQ], F32R)
        rl = sbuf(nc, ctx, "relu", [P, 2, SEQ])
        junk = sbuf(nc, ctx, "cmp_junk", [P, soff(NT)], mybir.dt.uint8)
        lath = sbuf(nc, ctx, "lat_hi", [P, 2, SEQ], F32R)
        latl = sbuf(nc, ctx, "lat_lo", [P, 2, SEQ], F32R)
        wkr = sbuf(nc, ctx, "wukv_raw", [P, 2, P])
        wks = sbuf(nc, ctx, "wukv", [P, 2, P])
        wkh = sbuf(nc, ctx, "wukv_hi", [P, 2, P], F32R)
        wkl = sbuf(nc, ctx, "wukv_lo", [P, 2, P], F32R)
        ssv = sbuf(nc, ctx, "kv_ssv", [P, NT])
        cnt = sbuf(nc, ctx, "cnt", [P, 8])
        need = sbuf(nc, ctx, "need", [P, 8])
        key = sbuf(nc, ctx, "key", [P, 8], I32)
        bit = sbuf(nc, ctx, "bit", [P, 8], I32)
        cand = sbuf(nc, ctx, "cand", [P, 8], I32)
        sg = sbuf(nc, ctx, "sg", [P, 8], I32)
        thr = sbuf(nc, ctx, "thr", [P, 8], I32)
        keep = sbuf(nc, ctx, "keep", [P, 8], I32)
        with ExitStack() as c:
            qis = sbuf(nc, c, "qidx_stack", [P, NIH, SEQ], F32R)
            kih = sbuf(nc, c, "kidx_hi2", [P, SEQ], F32R)
            kil = sbuf(nc, c, "kidx_lo2", [P, SEQ], F32R)
        with ExitStack() as c:
            gt = sbuf(nc, c, "gt", [P, SEQ])
            eq = sbuf(nc, c, "eq", [P, SEQ])
            cum = sbuf(nc, c, "cum", [P, SEQ])
        ps_p = psum(nc, ctx, "ps_proj", [P, 2, SEQ])
        ps_s = psum(nc, ctx, "ps_score", [P, 2, SEQ])

        raw_loaded = k.sems("win_loaded", 2)
        whi = k.sem("win_hi_ready")
        wlo = k.sem("win_lo_ready")
        proj = k.sem("proj_done")
        full = k.sem("proj_full_ready")
        hi = k.sem("proj_hi_ready")
        lo = k.sem("proj_lo_ready")
        spill = k.sems("proj_spilled", 2)
        wtr = k.sem("idxw_transposed")
        wtk = k.sem("idxw_ready")
        sqr = k.sem("lat_squared")
        zs = k.sem("idx_logits")
        rel = k.sem("idx_relu")
        scd = k.sem("score_summed")
        dgm = k.sem("diag_masked")
        kvw = k.sem("wukv_loaded")
        kvs = k.sem("wukv_scaled")
        kvh = k.sem("wukv_hi_ready")
        kvl = k.sem("wukv_lo_ready")
        ssm = k.sem("lat_ss_summed")
        ssn = k.sem("lat_ss_scaled")
        rkv = k.sem("lat_rstd_ready")
        kvp = k.sem("kv_projected")
        kvt = k.sem("kv_tok_ready")
        vdh = k.sem("vd_hi_ready")
        vdl = k.sem("vd_lo_ready")
        ktr = k.sem("kd_transposed")
        kfl = k.sem("kd_full_ready")
        kdh = k.sem("kd_hi_ready")
        kdl = k.sem("kd_lo_ready")
        kdup = k.sem("kd_doubled")
        tk = k.sem("topk_chain")
        sl = k.sem("select_chain")
        m01 = k.sem("first_blocks")

        w_in = A["w_in"][0].rearrange("(t p) n -> p t n", p=P)
        fixed = (C_IQ, C_IQ + P, C_IK, C_LAT, C_LAT + P)
        T_IKW, T_LAT, N1, NL = 2, 3, 5, 16
        units = [(i, h) for i in range(2, NT) for h in range(NIH)]
        base_spill = (128, 64)
        width = lambda n: IKW if n == T_IKW else P

        with nc.Block() as block:
            @block.sync
            def _(sp):
                def load(i, n):
                    if n >= 2:
                        sp.wait_ge(wlo, i + (n - 1))
                    c = fixed[n] if n < N1 else P * (n - N1)
                    src = w_in[:, :, bass.ds(i * P + c, P)] if n >= N1 else w_in[:, :, c:c + width(n)]
                    sp.dma_start(raw[:, n % 2, :, 0:width(n)], src).then_inc(raw_loaded[n % 2], 16)

                def stack_q(n):
                    for part, ready, top in ((evh, hi, 0), (evl, lo, HD)):
                        sp.wait_ge(ready, n + 1)
                        for j in range(2):
                            sp.dma_start(qis[top:top + HD, 2 * n + j, :].bitcast(F32),
                                         part[HD * j:HD * j + HD, n % 2].bitcast(F32)).then_inc(spill[n % 2], 16)

                def double_k():
                    for part, ready, dst in ((evh, hi, kih), (evl, lo, kil)):
                        sp.wait_ge(ready, T_IKW + 1)
                        for top in (0, HD):
                            sp.dma_start(dst[top:top + HD].bitcast(F32), part[0:HD, 0].bitcast(F32)).then_inc(spill[0], 16)

                def store(i, n):
                    for x, (part, ready) in enumerate(((evh, hi), (evl, lo))):
                        sp.wait_ge(ready, i + (n + 1))
                        sp.dma_start(scr[bass.ds(i + (n - N1), 1), x].rearrange("a p n -> (a p) n"),
                                     part[:, n % 2].bitcast(F32)).then_inc(spill[n % 2], 16)

                load(0, 0)
                load(0, 1)
                sp.dma_start(wkr[:, :, 0:HD], A["w_uk"][0].rearrange("(t p) n -> p t n", p=P)).then_inc(kvw, 16)
                sp.dma_start(wkr[:, :, HD:P], A["w_uv"][0].rearrange("(t p) n -> p t n", p=P)).then_inc(kvw, 16)
                load(0, 2)
                stack_q(0)
                load(0, 3)
                stack_q(1)
                load(0, 4)
                double_k()
                load(0, 5)
                load(0, 6)
                sp.wait_ge(kdl, 1)
                sp.dma_start(g.kdl[HD:P].bitcast(F32), g.kdl[0:HD].bitcast(F32)).then_inc(kdup, 16)
                with sp.Fori(0, NL - 2, 2) as i:
                    for j in range(2):
                        load(i, N1 + 2 + j)
                        store(i, N1 + j)
                for j in range(2):
                    store(NL - 2, N1 + j)
                sp.wait_ge(kdup, 16)
                for s in range(2):
                    sp.wait_ge(spill[s], base_spill[s] + 16 * NL)

            @block.scalar
            def _(act):
                def w_hi(i, n):
                    w = width(n)
                    act.wait_ge(raw_loaded[n % 2], i * 8 + 16 * (n // 2 + 1))
                    if n >= 2:
                        act.wait_ge(proj, i + (n - 1))
                    act.activation(wh[:, n % 2, :, 0:w], raw[:, n % 2, :, 0:w], ACT.Copy).then_inc(whi, 1)

                def evac(i, n, scale):
                    m = width(n)
                    act.wait_ge(proj, i + (n + 1))
                    if n >= 2:
                        act.wait_ge(lo, i + (n - 1))
                    act.activation(evf[0:m, n % 2], ps_p[0:m, n % 2], ACT.Copy, scale=scale).then_inc(full, 1)

                def e_hi(i, n, dst=None, spills=0):
                    m = width(n)
                    act.wait_ge(full, i + (n + 1))
                    if n >= N1 or spills:
                        act.wait_ge(spill[n % 2], i * 16 + spills)
                    act.activation(evh[0:m, n % 2] if dst is None else dst, evf[0:m, n % 2], ACT.Copy).then_inc(hi, 1)

                w_hi(0, 0)
                w_hi(0, 1)
                for n in range(3):
                    w_hi(0, n + 2)
                    evac(0, n, 0.125 if n < 2 else 1.0)
                    e_hi(0, n, spills=64 * (n == 2))
                act.wait_ge(wtr, 1)
                act.activation(g.wtok[:], ps_s[:, 0, 0:NIH * NT].rearrange("p (a b) -> p a b", b=NIH),
                               ACT.Copy, scale=0.5).then_inc(wtk, 1)
                act.wait_ge(kvw, 32)
                for t in range(2):
                    act.activation(wks[:, t], wkr[:, t], ACT.Copy, scale=g.cols[:, R_KV + t:R_KV + t + 1]).then_inc(kvs, 1)
                act.wait_ge(kvs, 2)
                act.activation(wkh[:], wks[:], ACT.Copy).then_inc(kvh, 1)
                w_hi(0, 5)
                evac(0, T_LAT, 1.0)
                e_hi(0, T_LAT, dst=lath[:, 0])
                for u, (i, h) in enumerate(units):
                    w = P * (i + 1)
                    act.wait_ge(zs, u + 1)
                    if u >= 2:
                        act.wait_ge(scd, u - 1)
                    act.activation(rl[:, u % 2, 0:w], ps_s[:, u % 2, 0:w], ACT.Relu).then_inc(rel, 1)
                w_hi(0, 6)
                evac(0, T_LAT + 1, 1.0)
                e_hi(0, T_LAT + 1, dst=lath[:, 1])
                for t in range(2):
                    act.wait_ge(scd, len(units) - 1 + t)
                    act.activation(rl[:, t], evf[:, (T_LAT + t) % 2], ACT.Square).then_inc(sqr, 1)
                act.wait_ge(ssm, 1)
                act.activation(ssv[:], ps_s[:, 0, 0:NT], ACT.Copy, scale=1.0 / KV).then_inc(ssn, 1)
                act.wait_ge(kvp, 1)
                act.wait_ge(rkv, 1)
                for i in range(NT):
                    act.activation(rl[:, 0, P * i:P * i + P], ps_s[:, 1, P * i:P * i + P], ACT.Copy,
                                   scale=g.rkv[:, i:i + 1]).then_inc(kvt, 1)
                act.wait_ge(kvt, NT)
                act.activation(g.vd[:, :, 0:HD], rl[:, 0].rearrange("p (b d) -> p b d", b=NT)[:, :, HD:P],
                               ACT.Copy).then_inc(vdh, 1)
                act.wait_ge(ktr, 1)
                act.activation(rl[0:HD, 1], ps_s[0:HD, 0], ACT.Copy).then_inc(kfl, 1)
                for top in (0, HD):
                    act.activation(g.kdh[top:top + HD], ps_s[0:HD, 0], ACT.Copy).then_inc(kdh, 1)

                def step(i, j):
                    evac(i, N1 + j, g.qscale[:, bass.ds(i + j, 1)])
                    e_hi(i, N1 + j, spills=base_spill[(N1 + j) % 2])
                with act.Fori(0, NL - 2, 2) as i:
                    for j in range(2):
                        w_hi(i, N1 + 2 + j)
                        step(i, j)
                for j in range(2):
                    step(NL - 2, j)

            @block.gpsimd
            def _(pool):
                def w_lo(i, n):
                    w = width(n)
                    pool.wait_ge(whi, i + (n + 1))
                    if n >= 2:
                        pool.wait_ge(proj, i + (n - 1))
                    pool.tensor_tensor(wl[:, n % 2, :, 0:w], raw[:, n % 2, :, 0:w],
                                       wh[:, n % 2, :, 0:w].bitcast(F32), ALU.subtract).then_inc(wlo, 1)

                def e_lo(i, n, dst=None, high=None, spills=0):
                    m = width(n)
                    pool.wait_ge(hi, i + (n + 1))
                    if n >= N1 or spills:
                        pool.wait_ge(spill[n % 2], i * 16 + spills)
                    pool.tensor_tensor(evl[0:m, n % 2] if dst is None else dst, evf[0:m, n % 2],
                                       (evh[0:m, n % 2] if high is None else high).bitcast(F32),
                                       ALU.subtract).then_inc(lo, 1)

                w_lo(0, 0)
                w_lo(0, 1)
                for n in range(3):
                    w_lo(0, n + 2)
                    e_lo(0, n, spills=64 * (n == 2))
                pool.wait_ge(kvh, 1)
                pool.tensor_tensor(wkl[:], wks[:], wkh[:].bitcast(F32), ALU.subtract).then_inc(kvl, 1)
                w_lo(0, 5)
                e_lo(0, T_LAT, dst=latl[:, 0], high=lath[:, 0])
                for i in range(2):
                    s = g.score[:, soff(i):soff(i + 1)]
                    pool.tensor_copy(s, g.dist[:, SEQ - P * (i + 1):SEQ]).then_inc(m01, 1)
                for i in range(NT):
                    if i < 2:
                        pool.wait_ge(m01, i + 1)
                    else:
                        pool.wait_ge(scd, NIH * (i - 1))
                    s = g.score[:, soff(i + 1) - P:soff(i + 1)]
                    pool.affine_select(out=s, in_=s, compare_op=ALU.is_ge, fill=-BIG if i < 2 else -3e38,
                                       base=0, pattern=[[-1, P]], channel_multiplier=1).then_inc(dgm, 1)
                w_lo(0, 6)
                e_lo(0, T_LAT + 1, dst=latl[:, 1], high=lath[:, 1])
                pool.wait_ge(ssn, 1)
                pool.tensor_scalar(ssv[:], ssv[:], 1.0, EPS, ALU.mult, ALU.add).then_inc(ssn, 1)
                pool.wait_ge(ssn, 2)
                pool.tensor_tensor(g.rkv[:], ssv[:], g.nhalf[:], ALU.pow).then_inc(rkv, 1)
                pool.wait_ge(vdh, 1)
                pool.tensor_tensor(g.vd[:, :, HD:P], rl[:, 0].rearrange("p (b d) -> p b d", b=NT)[:, :, HD:P],
                                   g.vd[:, :, 0:HD].bitcast(F32), ALU.subtract).then_inc(vdl, 1)
                pool.wait_ge(kfl, 1)
                pool.wait_ge(kdh, 1)
                pool.tensor_tensor(g.kdl[0:HD], rl[0:HD, 1], g.kdh[0:HD].bitcast(F32), ALU.subtract).then_inc(kdl, 1)
                with pool.Fori(0, NL - 2, 2) as i:
                    for j in range(2):
                        w_lo(i, N1 + 2 + j)
                        e_lo(i, N1 + j, spills=base_spill[(N1 + j) % 2])
                for j in range(2):
                    e_lo(NL - 2, N1 + j, spills=base_spill[(N1 + j) % 2])

            @block.tensor
            def _(pe):
                def project(i, n):
                    pe.wait_ge(wlo, i + (n + 1))
                    if n >= 2:
                        pe.wait_ge(full, i + (n - 1))
                    s, m = n % 2, width(n)
                    tile_products(pe, ps_p[0:m, s], wh[:, s, :, 0:m], wl[:, s, :, 0:m], g.hTh, g.hTl).then_inc(proj, 1)

                for n in range(3):
                    project(0, n)
                pe.wait_ge(full, T_IKW + 1)
                for i in range(NT):
                    last = pe.transpose(ps_s[:, 0, NIH * i:NIH * i + NIH], evf[HD:IKW, 0, P * i:P * i + P],
                                        g.ident[HD:IKW, HD:IKW])
                last.then_inc(wtr, 1)
                project(0, T_LAT)
                pe.wait_ge(wtk, 1)
                pe.wait_ge(spill[0], 128)
                pe.wait_ge(spill[1], 64)
                for u, (i, h) in enumerate(units):
                    if u >= 2:
                        pe.wait_ge(rel, u - 1)
                    w = P * (i + 1)
                    for c in range(0, w, HALF):
                        s = slice(c, min(c + HALF, w))
                        q = qis[:, h, P * i:P * i + P]
                        pe.matmul(ps_s[:, u % 2, s], q, kih[:, s], start=True, stop=False)
                        last = pe.matmul(ps_s[:, u % 2, s], q, kil[:, s], start=False, stop=True)
                    last.then_inc(zs, 1)
                project(0, T_LAT + 1)
                pe.wait_ge(sqr, 2)
                pe.wait_ge(rel, len(units))
                for i in range(NT):
                    for t in range(2):
                        last = pe.matmul(ps_s[:, 0, i:i + 1], rl[:, t, P * i:P * i + P], g.ones[:, 0:1],
                                         start=(t == 0), stop=(t == 1))
                last.then_inc(ssm, 1)
                pe.wait_ge(kvl, 1)
                pe.wait_ge(lo, T_LAT + 2)
                for i in range(NT):
                    for t in range(2):
                        for x, w in ((lath, wkh), (lath, wkl), (latl, wkh)):
                            last = pe.matmul(ps_s[:, 1, P * i:P * i + P], x[:, t, P * i:P * i + P], w[:, t],
                                             start=(t == 0 and x is lath and w is wkh), stop=(t == 1 and x is latl))
                last.then_inc(kvp, 1)
                pe.wait_ge(kvt, NT)
                for i in range(NT):
                    last = pe.transpose(ps_s[:, 0, P * i:P * i + P], rl[:, 0, P * i:P * i + P], g.ident[:])
                last.then_inc(ktr, 1)
                with pe.Fori(0, NL, 2) as i:
                    for j in range(2):
                        project(i, N1 + j)

            @block.vector
            def _(dve):
                for u, (i, h) in enumerate(units):
                    w = P * (i + 1)
                    s = g.score[:, soff(i):soff(i + 1)]
                    dve.wait_ge(rel, u + 1)
                    if h == 0:
                        dve.tensor_scalar(s, rl[:, u % 2, 0:w], g.wtok[:, i, 0:1], None, ALU.mult).then_inc(scd, 1)
                    else:
                        dve.wait_ge(scd, u)
                        dve.scalar_tensor_tensor(out=s, in0=rl[:, u % 2, 0:w], scalar=g.wtok[:, i, h:h + 1], in1=s,
                                                 op0=ALU.mult, op1=ALU.add).then_inc(scd, 1)
                dve.memset(bit[:], 1 << 30).then_inc(tk, 1)
                dve.wait_ge(dgm, NT)

                def counts(at, done):
                    for i in range(2, NT):
                        w = slice(soff(i), soff(i + 1))
                        last = dve.tensor_scalar(junk[:, w], g.score[:, w], at(i - 2), None, ALU.is_ge, ALU.add,
                                                 accum_out=cnt[:, i - 2:i - 1])
                    last.then_inc(done, 1)

                NB = NT - 2
                b = slice(0, NB)
                counts(lambda i: 0.0, tk)
                dve.wait_ge(tk, 2)
                dve.tensor_scalar(key[:, b], cnt[:, b], float(TOPK), -2.0 ** 31, ALU.is_lt, ALU.mult).then_inc(tk, 1)

                with dve.Fori(0, 31) as n:
                    dve.wait_ge(tk, n * 8 + 3)
                    dve.tensor_tensor(cand[:, b], key[:, b], bit[:, b], ALU.bitwise_or).then_inc(tk, 1)
                    dve.wait_ge(tk, n * 8 + 4)
                    dve.tensor_scalar(sg[:, b], cand[:, b], 31, 0x7FFFFFFF, ALU.arith_shift_right,
                                      ALU.bitwise_and).then_inc(tk, 1)
                    dve.wait_ge(tk, n * 8 + 5)
                    dve.tensor_tensor(thr[:, b], cand[:, b], sg[:, b], ALU.bitwise_xor).then_inc(tk, 1)
                    dve.wait_ge(tk, n * 8 + 6)
                    counts(lambda i: thr[:, i:i + 1].bitcast(F32), tk)
                    dve.wait_ge(tk, n * 8 + 7)
                    dve.tensor_scalar(keep[:, b], cnt[:, b], float(TOPK), -1.0, ALU.is_ge, ALU.mult).then_inc(tk, 1)
                    dve.wait_ge(tk, n * 8 + 8)
                    dve.tensor_tensor(keep[:, b], keep[:, b], bit[:, b], ALU.bitwise_and).then_inc(tk, 1)
                    dve.wait_ge(tk, n * 8 + 9)
                    dve.tensor_tensor(key[:, b], key[:, b], keep[:, b], ALU.bitwise_or).then_inc(tk, 1)
                    dve.tensor_scalar(bit[:, b], bit[:, b], 1, None, ALU.logical_shift_right).then_inc(tk, 1)
                dve.wait_ge(tk, 31 * 8 + 3)
                dve.tensor_scalar(sg[:, b], key[:, b], 31, 0x7FFFFFFF, ALU.arith_shift_right,
                                  ALU.bitwise_and).then_inc(tk, 1)
                dve.wait_ge(tk, 31 * 8 + 4)
                dve.tensor_tensor(thr[:, b], key[:, b], sg[:, b], ALU.bitwise_xor).then_inc(tk, 1)
                dve.wait_ge(tk, 31 * 8 + 5)
                done = [0]

                def then(ins):
                    ins.then_inc(sl, 1)
                    done[0] += 1
                    dve.wait_ge(sl, done[0])

                for i in range(2, NT):
                    w = P * (i + 1)
                    s = g.score[:, soff(i):soff(i + 1)]
                    t = thr[:, i - 2:i - 1].bitcast(F32)
                    o = slice(i - 2, i - 1)
                    dve.tensor_scalar(gt[:, 0:w], s, t, None, ALU.is_gt, ALU.add, accum_out=cnt[:, o])
                    then(dve.tensor_scalar(eq[:, 0:w], s, t, None, ALU.is_equal))
                    dve.tensor_scalar(need[:, o], cnt[:, o], -1.0, float(TOPK), ALU.mult, ALU.add)
                    then(dve.tensor_tensor_scan(cum[:, 0:w], eq[:, 0:w], eq[:, 0:w], 0.0, ALU.add, ALU.max))
                    then(dve.scalar_tensor_tensor(out=eq[:, 0:w], in0=cum[:, 0:w], scalar=need[:, o],
                                                  in1=eq[:, 0:w], op0=ALU.is_le, op1=ALU.mult))
                    then(dve.tensor_tensor(gt[:, 0:w], gt[:, 0:w], eq[:, 0:w], ALU.add))
                    then(dve.tensor_scalar(gt[:, 0:w], gt[:, 0:w], -1.0, BIG, ALU.add, ALU.mult))
                    then(dve.tensor_tensor(s, gt[:, 0:w], g.dist[:, SEQ - w:SEQ], ALU.add))


def phase2(nc, k, g, scr):
    GRP = [[(G, b) for b in range(4 * G + 3, -1, -1)] for G in range(2)]
    HU = sum(len(x) for x in GRP)
    NU = 2 * HU
    units = [(j, G, b) for j in range(2) for grp in GRP for G, b in grp]
    off = lambda G, b: P * max(0, b - 4 * G)
    first = {}
    n = 0
    for G in range(2):
        for b in range(4 * G + 4):
            first[G, b] = n - off(G, b)
            n += HALF - off(G, b)
    diag = [b >= 4 * G for j, G, b in units]
    ZS = 5
    with ExitStack() as ctx:
        qh = sbuf(nc, ctx, "sb_q_hi2", [P, 2, SEQ], F32R)
        ql = sbuf(nc, ctx, "sb_q_lo2", [P, 2, SEQ], F32R)
        ks = sbuf(nc, ctx, "sb_k_stack", [P, 2, SEQ], F32R)
        vt = sbuf(nc, ctx, "sb_vT_stack", [P, 2, SEQ])
        vs = sbuf(nc, ctx, "sb_v", [P, 2, NT, P], F32R)
        ph = sbuf(nc, ctx, "sp_hi", [P, n], F32R)
        pl = sbuf(nc, ctx, "sp_lo", [P, n], F32R)
        e = sbuf(nc, ctx, "exp_z", [P, 2, HALF])
        sp_ = sbuf(nc, ctx, "softplus", [P, 2, HALF])
        a = sbuf(nc, ctx, "a_full", [P, 2, HALF])
        ah = sbuf(nc, ctx, "a_hi", [P, 2, HALF], F32R)
        al = sbuf(nc, ctx, "a_lo", [P, 2, HALF], F32R)
        tmp = sbuf(nc, ctx, "o_lo_part", [HD, 2, HALF])
        z = psum(nc, ctx, "ps_z", [P, ZS, HALF])
        o = psum(nc, ctx, "ps_o", [P, 2, HALF])
        tv = psum(nc, ctx, "ps_vt", [P, HALF])

        loaded = k.sems("sb_loaded", 2)
        v_tr = k.sem("sb_v_transposed")
        v_rdy = k.sem("sb_v_ready")
        z_rdy = k.sem("z_ready")
        cl = k.sem("z_clamped")
        ex = k.sem("z_exp")
        ln = k.sem("z_ln")
        mx = k.sem("softplus_ready")
        phr = k.sem("sp_hi_ready")
        plr = k.sem("sp_lo_ready")
        cum = k.sem("sums_added")
        ar = k.sem("a_ready")
        ahr = k.sem("a_hi_ready")
        alr = k.sem("a_lo_ready")
        vd = k.sem("o_added")
        tm = k.sem("o_lo_out")
        od = k.sem("o_stored")

        def at(u):
            return 0 <= u < NU

        def sl(u):
            j, G, b = units[u]
            return slice(off(G, b), HALF)

        def psl(u):
            j, G, b = units[u]
            return slice(first[G, b] + off(G, b), first[G, b] + HALF)

        def group_end(u):
            return units[u][2] == 0

        with nc.Block() as block:
            @block.sync
            def _(sp):
                scr2 = scr.rearrange("t x p n -> (t x p) n")

                def load(i, ahead, j):
                    for dst, t0, parts in ((qh, 0, (0, 0)), (ql, 0, (1, 1)), (ks, 4, (0, 1)), (vt, 8, (0, 1))):
                        for x in range(2):
                            d = dst[HD * x:HD * x + HD, j]
                            r = (2 * t0 + ahead + parts[x]) * P + HD * j
                            src = scr2[r:r + HD, :] if i is None else scr2[bass.ds(i * P + r, HD), :]
                            sp.dma_start(d if dst is vt else d.bitcast(F32), src).then_inc(loaded[j], 16)

                load(None, 0, 0)
                load(None, 0, 1)
                with sp.Fori(0, NH - 2, 2) as i:
                    for j in range(2):
                        sp.wait_ge(vd, i * HU + (HU * (j + 1) + 2))
                        load(i, 2, j)

            @block.scalar
            def _(act):
                act.sem_inc(ar, ZS)
                act.preload_act_table_set("natural_log_exp_and_others")
                with act.Fori(0, NH // 2) as it:
                    def step(s):
                        if s in (0, HU):
                            j = s // HU
                            for x in range(2):
                                act.wait_ge(v_tr, it * 4 + (2 * j + x + 1))
                                act.activation(vs[:, j, 4 * x:4 * x + 4, :], tv[:].rearrange("p (b d) -> p b d", b=4),
                                               ACT.Copy).then_inc(v_rdy, 1)
                        u = s
                        if at(u):
                            act.wait_ge(cl, it * NU + (u + 1))
                            act.activation(e[:, u % 2, sl(u)], e[:, u % 2, sl(u)], ACT.Exp).then_inc(ex, 1)
                        u = s - 3
                        if at(u):
                            act.wait_ge(cum, it * NU + (u + 6))
                            act.wait_ge(alr, it * NU + (u + 1))
                            act.activation(a[:, u % 2, sl(u)], z[:, u % ZS, sl(u)], ACT.Exp).then_inc(ar, 1)
                        u = s
                        if at(u):
                            act.wait_ge(ex, it * NU + (u + 1))
                            act.activation(e[:, u % 2, sl(u)], e[:, u % 2, sl(u)], ACT.Ln, bias=1.0).then_inc(ln, 1)
                        u = s - 5
                        if at(u) and group_end(u):
                            q = sum(group_end(x) for x in range(u))
                            act.wait_ge(vd, it * NU + (u + 3))
                            act.wait_ge(od, it * 4 + (q + 1))
                            act.activation(tmp[:, q % 2], o[HD:P, q % 2], ACT.Copy).then_inc(tm, 1)
                    for s in range(NU + 5):
                        step(s)

            @block.gpsimd
            def _(pool):
                pool.sem_inc(plr, 2)
                pool.sem_inc(alr, 2)
                with pool.Fori(0, NH // 2) as it:
                    for s in range(NU + 4):
                        u = s - 1
                        if at(u):
                            pool.wait_ge(phr, it * NU + (u + 1))
                            pool.tensor_tensor(pl[:, psl(u)], sp_[:, u % 2, sl(u)], ph[:, psl(u)].bitcast(F32),
                                               ALU.subtract).then_inc(plr, 1)
                        u = s - 4
                        if at(u):
                            pool.wait_ge(ahr, it * NU + (u + 1))
                            pool.wait_ge(vd, it * NU + (u + 1))
                            pool.tensor_tensor(al[:, u % 2, sl(u)], a[:, u % 2, sl(u)], ah[:, u % 2, sl(u)].bitcast(F32),
                                               ALU.subtract).then_inc(alr, 1)

            @block.vector
            def _(dve):
                dve.sem_inc(mx, 2)
                dve.sem_inc(od, 2)
                with dve.Fori(0, NH // 2) as it:
                    for s in range(NU + 6):
                        u = s
                        if at(u):
                            dve.wait_ge(z_rdy, it * NU + (u + 1))
                            dve.wait_ge(mx, it * NU + (u + 1))
                            dve.tensor_scalar(e[:, u % 2, sl(u)], z[:, u % ZS, sl(u)], ZCLAMP, None, ALU.min).then_inc(cl, 1)
                        u = s - 1
                        if at(u):
                            dve.wait_ge(ln, it * NU + (u + 1))
                            dve.wait_ge(plr, it * NU + (u + 1))
                            dve.tensor_tensor(sp_[:, u % 2, sl(u)], z[:, u % ZS, sl(u)], e[:, u % 2, sl(u)],
                                              ALU.max).then_inc(mx, 1)
                        u = s - 4
                        if at(u):
                            dve.wait_ge(ar, it * NU + (u + 1 + ZS))
                            dve.wait_ge(vd, it * NU + (u + 1))
                            dve.tensor_copy(ah[:, u % 2, sl(u)], a[:, u % 2, sl(u)]).then_inc(ahr, 1)
                        u = s - 1
                        if at(u):
                            dve.wait_ge(mx, it * NU + (u + 3))
                            dve.wait_ge(cum, it * NU + (u + 1))
                            dve.tensor_copy(ph[:, psl(u)], sp_[:, u % 2, sl(u)]).then_inc(phr, 1)
                        u = s - 5
                        if at(u) and group_end(u):
                            q = sum(group_end(x) for x in range(u))
                            j, G, b = units[u]
                            dve.wait_ge(tm, it * 4 + (q + 1))
                            dve.tensor_tensor(g.osb[HD * j:HD * j + HD, bass.ds(it, 1), HALF * G:HALF * G + HALF]
                                              .rearrange("p a n -> p (a n)"), o[0:HD, q % 2], tmp[:, q % 2],
                                              ALU.add).then_inc(od, 1)

            @block.tensor
            def _(pe):
                pe.sem_inc(v_rdy, 1)
                pe.sem_inc(cum, 5)
                pe.sem_inc(vd, 2)
                with pe.Fori(0, NH // 2) as it:
                    for s in range(NU + 4):
                        if s in (0, HU):
                            j = s // HU
                            pe.wait_ge(loaded[j], it * 128 + 128)
                            for x in range(2):
                                pe.wait_ge(v_rdy, it * 4 + (2 * j + x + 1))
                                for b in range(4):
                                    last = pe.transpose(tv[:, P * b:P * b + P],
                                                        vt[:, j, P * (4 * x + b):P * (4 * x + b) + P], g.ident[:])
                                last.then_inc(v_tr, 1)
                        u = s
                        if at(u):
                            j, G, b = units[u]
                            pe.wait_ge(ar, it * NU + (u + 1))
                            q = slice(HALF * G + off(G, b), HALF * G + HALF)
                            kb = ks[:, j, P * b:P * b + P]
                            pe.matmul(z[:, u % ZS, sl(u)], kb, qh[:, j, q], start=True, stop=False)
                            last = pe.matmul(z[:, u % ZS, sl(u)], kb, ql[:, j, q], start=False, stop=True)
                            if diag[u]:
                                d = slice(off(G, b), off(G, b) + P)
                                last = pe.matmul(z[:, u % ZS, d], g.bigid[:], g.tneg[:], start=False, stop=True,
                                                 skip_group_check=True)
                            last.then_inc(z_rdy, 1)
                        u = s - 2
                        if at(u):
                            j, G, b = units[u]
                            pe.wait_ge(plr, it * NU + (u + 3))
                            for c in range(4 * G + 3, b - 1, -1):
                                w = g.tneg if c == b else g.nneg
                                s_ = slice(off(G, c), HALF)
                                for part in (ph, pl):
                                    last = pe.matmul(z[:, u % ZS, s_], w[:], part[:, first[G, c] + off(G, c):first[G, c] + HALF],
                                                     start=False, stop=(c == b and part is pl), skip_group_check=True)
                            last.then_inc(cum, 1)
                        u = s - 4
                        if at(u):
                            j, G, b = units[u]
                            q = sum(group_end(x) for x in range(u))
                            pe.wait_ge(alr, it * NU + (u + 3))
                            if b == 4 * G + 3:
                                pe.wait_ge(od, it * 4 + (q + 1))
                                pe.wait_ge(v_rdy, it * 4 + (2 * j + 3))
                            for part in (ah, al):
                                last = pe.matmul(o[:, q % 2, sl(u)], vs[:, j, b], part[:, u % 2, sl(u)],
                                                 start=(b == 4 * G + 3 and part is ah), stop=(b == 0 and part is al),
                                                 skip_group_check=True)
                            last.then_inc(vd, 1)


def phase3(nc, k, g, A, scr, vecs):
    chunks = []
    units = []
    for j in range(2):
        for i in range(NT - 1, -1, -1):
            for c in range(0, i + 1, 4):
                chunks.append((len(units), j, i, c, min(4, i + 1 - c)))
            units.append((j, i))
    NU, NC = len(units), len(chunks)
    last_chunk = [max(q for q in range(NC) if chunks[q][0] == u) for u in range(NU)]
    TS = 3
    with ExitStack() as ctx:
        qs = sbuf(nc, ctx, "d_q_stack", [P, 2, SEQ], F32R)
        nl = sbuf(nc, ctx, "neg_logits", [P, 2, SEQ])
        pe_ = sbuf(nc, ctx, "probs", [P, 2, SEQ])
        th = sbuf(nc, ctx, "pT_hi", [P, TS, HALF], F32R)
        tl = sbuf(nc, ctx, "pT_lo", [P, TS, HALF], F32R)
        nm = sbuf(nc, ctx, "neg_max", [P, 2])
        sm = sbuf(nc, ctx, "prob_sum", [P, 4])
        rs = sbuf(nc, ctx, "prob_rsum", [P, 2])
        ns = sbuf(nc, ctx, "head_nslope", [P, 2])
        tmp = sbuf(nc, ctx, "od_lo_part", [P, 2, HD])
        wm = sbuf(nc, ctx, "wmod_b", [P, 2, KD, 512])
        acc = sbuf(nc, ctx, "mod_acc_b", [P, 12, 512])
        prod = sbuf(nc, ctx, "mod_prod", [P, 2, 512])
        row = sbuf(nc, ctx, "mod_rows", [1, 5, D])
        mb = sbuf(nc, ctx, "mb2", [P, 16])
        z = psum(nc, ctx, "ps_dz", [P, 2, SEQ])
        tr = psum(nc, ctx, "ps_dt", [P, 2, HALF])
        o = psum(nc, ctx, "ps_do", [P, 2, HALF])

        loaded = k.sems("d_loaded", 2)
        zr = k.sem("dz_ready")
        nsr = k.sem("d_slope_ready")
        seen = k.sem("dz_seen")
        tt = k.sem("neg_logits_ready")
        ex = k.sem("probs_ready")
        td = k.sem("p_transposed")
        thr = k.sem("pT_hi_ready")
        tlr = k.sem("pT_lo_ready")
        vd = k.sem("d_o_added")
        rc = k.sem("d_rsum_ready")
        f1 = k.sem("d_lo_out")
        oo = k.sem("d_o_stored")

        wm_loaded = k.sems("wmb_loaded", 2)
        row_loaded = k.sem("row_bias_loaded")
        chain = k.sem("modb_first_product")
        pr = k.sem("modb_product")
        summed = k.sem("modb_summed")
        accd = k.sem("modb_acc_done")
        colm = k.sem("mod2_summed")
        rowm = k.sem("row_summed")
        mbs = k.sem("mod2_biased")
        rowd = k.sem("row_ready")
        row_stored = k.sem("row_stored")
        mods = [(A["w_mod"][0], 2 * D + 512 * c) for c in range(8)] + [(A["w_mod_final"], 512 * c) for c in range(4)]
        rows = [(0, 0, 0, tr[0:1, 0]), (1, 0, 1, tr[0:1, 1]), (6, 1, 0, z[0:1, 0, HALF:]), (7, 1, 1, z[0:1, 1, 0:HALF]),
                (8, 2, 0, z[0:1, 1, HALF:]), (9, 2, 1, o[0:1, 0]), (10, 3, 0, o[0:1, 1]), (11, 3, 1, z[0:1, 0, 0:HALF])]
        STEPS = NH // 2

        def of(u):
            return [q for q in range(NC) if chunks[q][0] == u]

        with nc.Block() as block:
            @block.sync
            def _(sp):
                scr2 = scr.rearrange("t x p n -> (t x p) n")

                def load(i, row, j):
                    for x in range(2):
                        r = (12 * 2 + x) * P + HD * j + row
                        src = scr2[r:r + HD, :] if i is None else scr2[bass.ds(i * 2 * P + r, HD), :]
                        sp.dma_start(qs[HD * x:HD * x + HD, j].bitcast(F32), src).then_inc(loaded[j], 16)

                for j in range(2):
                    load(None, 0, j)

                def load_mod(c):
                    if c >= 2:
                        sp.wait_ge(accd, c - 1)
                    w, col = mods[c]
                    sp.dma_start(wm[:, c % 2], w.rearrange("(t p) n -> p t n", p=P)[:, :, col:col + 512])\
                      .then_inc(wm_loaded[c % 2], 16)

                for r, b in enumerate((A["b_mod"][0:1, 2 * D:3 * D], A["b_mod"][0:1, 5 * D:6 * D],
                                       A["b_mod_final"][0:D].unsqueeze(0), A["b_mod_final"][D:2 * D].unsqueeze(0),
                                       A["final_gain"].unsqueeze(0))):
                    sp.dma_start(row[:, r], b).then_inc(row_loaded, 16)
                for h in range(2, NH):
                    for c in (2 * h - 4, 2 * h - 3):
                        load_mod(c)
                    sp.wait_ge(zr, NT * (h - 1))
                    load(None, (h // 2) * 2 * P, h % 2)
                sp.wait_ge(rowd, 10)
                sp.dma_start(vecs.rearrange("(o r) n -> o r n", o=1), row[:, 0:4]).then_inc(row_stored, 16)
                sp.wait_ge(row_stored, 16)

            @block.gpsimd
            def _(pool):
                for c in range(12):
                    pool.wait_ge(wm_loaded[c % 2], 16 * (c // 2 + 1))
                    pool.tensor_scalar(acc[:, c], wm[:, c % 2, 0], g.csil[:, 0:1], None, ALU.mult).then_inc(chain, 1)
                    for t in range(1, KD):
                        n = 7 * c + t - 1
                        if n >= 2:
                            pool.wait_ge(summed, n - 1)
                        pool.tensor_scalar(prod[:, n % 2], wm[:, c % 2, t], g.csil[:, t:t + 1], None, ALU.mult)\
                            .then_inc(pr, 1)
                        pool.wait_ge(pr, n + 1)
                        if t == 1:
                            pool.wait_ge(chain, c + 1)
                        else:
                            pool.wait_ge(summed, n)
                        ins = pool.tensor_tensor(acc[:, c], acc[:, c], prod[:, n % 2], ALU.add)
                        ins.then_inc(summed, 1)
                    pool.wait_ge(summed, 7 * c + 7)
                    pool.sem_inc(accd, 1)

            @block.scalar
            def _(act):
                act.sem_inc(ex, 2)
                with act.Fori(0, NH // 2) as it:
                    def fin(u):
                        act.wait_ge(rc, it * NU + (u + 1))
                        act.wait_ge(vd, it * NC + (last_chunk[u] + 1 + TS))
                        act.activation(tmp[:, u % 2], o[:, u % 2, HD:P], ACT.Copy,
                                       scale=rs[:, u % 2:u % 2 + 1]).then_inc(f1, 1)

                    for s in range(NU + 2):
                        if s < NU:
                            j, i = units[s]
                            w = P * (i + 1)
                            act.wait_ge(tt, it * NU + (s + 3))
                            act.wait_ge(td, it * NC + (last_chunk[s - 2] + 2 if s >= 2 else 1))
                            act.activation(pe_[:, s % 2, 0:w], nl[:, s % 2, 0:w], ACT.Exp, scale=-1.0,
                                           bias=nm[:, s % 2:s % 2 + 1], accum_out=sm[:, s % 4:s % 4 + 1]).then_inc(ex, 1)
                        for n, q in enumerate(of(s - 1)):
                            w = P * chunks[q][4]
                            act.wait_ge(td, it * NC + (q + 2))
                            act.wait_ge(vd, it * NC + (q + 1))
                            act.activation(th[:, q % TS, 0:w], tr[:, q % 2, 0:w], ACT.Copy).then_inc(thr, 1)
                            if n == 0 and s >= 2:
                                fin(s - 2)
                        if s == NU + 1:
                            fin(s - 2)

            @block.vector
            def _(dve):
                dve.sem_inc(tt, 2)
                dve.sem_inc(tlr, 2)
                dve.sem_inc(oo, 2)
                with dve.Fori(0, NH // 2) as it:
                    for j in range(2):
                        dve.wait_ge(tt, it * NU + 2)
                        dve.tensor_copy(ns[:, j:j + 1], g.nslope[:, bass.ds(it * 2 + j, 1)]).then_inc(nsr, 1)
                    dve.wait_ge(nsr, it * 2 + 2)

                    def finish(u):
                        j, i = units[u]
                        dve.wait_ge(f1, it * NU + (u + 1))
                        dve.scalar_tensor_tensor(out=g.otok[:, i, bass.ds(it * P + HD * j, HD)], in0=o[:, u % 2, 0:HD],
                                                 scalar=rs[:, u % 2:u % 2 + 1], in1=tmp[:, u % 2], op0=ALU.mult,
                                                 op1=ALU.add).then_inc(oo, 1)
                    for s in range(NU + 2):
                        if s < NU:
                            j, i = units[s]
                            w = P * (i + 1)
                            dve.wait_ge(zr, it * NU + (s + 1))
                            dve.wait_ge(ex, it * NU + (s + 1))
                            dve.sem_inc(seen, 1)
                            dve.tensor_tensor_reduce(nl[:, s % 2, 0:w], z[:, s % 2, 0:w], g.score[:, soff(i):soff(i + 1)],
                                                     ns[:, j:j + 1], 3e38, ALU.add, ALU.min,
                                                     nm[:, s % 2:s % 2 + 1]).then_inc(tt, 1)
                        for n, q in enumerate(of(s - 1)):
                            w = P * chunks[q][4]
                            dve.wait_ge(thr, it * NC + (q + 1))
                            dve.tensor_tensor(tl[:, q % TS, 0:w], tr[:, q % 2, 0:w], th[:, q % TS, 0:w].bitcast(F32),
                                              ALU.subtract).then_inc(tlr, 1)
                            if n == 0 and s >= 2:
                                finish(s - 2)
                        if s == NU + 1:
                            finish(s - 2)
                        u = s - 1
                        if 0 <= u < NU:
                            dve.wait_ge(ex, it * NU + (u + 3))
                            dve.wait_ge(oo, it * NU + (u + 1))
                            dve.reciprocal(rs[:, u % 2:u % 2 + 1], sm[:, u % 4:u % 4 + 1]).then_inc(rc, 1)
                dve.wait_ge(colm, 1)
                dve.tensor_tensor(mb[:], z[:, 0, 0:16], g.cols[:, 24:40], ALU.add).then_inc(mbs, 1)
                dve.wait_ge(mbs, 1)
                dve.tensor_copy(g.b2[:], mb[:, 0:8]).then_inc(mbs, 1)
                dve.scalar_tensor_tensor(out=g.a2[:], in0=mb[:, 8:16], scalar=1.0, in1=g.cols[:, R_N2:R_N2 + 8],
                                         op0=ALU.add, op1=ALU.mult).then_inc(mbs, 1)
                dve.wait_ge(row_loaded, 16 * 5)
                for n, (c, r, half, ps) in enumerate(rows):
                    x = slice(HALF * half, HALF * half + HALF)
                    dve.wait_ge(rowm, n + 1)
                    dve.tensor_tensor(row[:, r, x], ps, row[:, r, x], ALU.add).then_inc(rowd, 1)
                dve.wait_ge(rowd, len(rows))
                for half in range(2):
                    x = slice(HALF * half, HALF * half + HALF)
                    dve.scalar_tensor_tensor(out=row[:, 3, x], in0=row[:, 3, x], scalar=1.0, in1=row[:, 4, x],
                                             op0=ALU.add, op1=ALU.mult).then_inc(rowd, 1)

            @block.tensor
            def _(pe):
                pe.sem_inc(vd, TS)
                pe.sem_inc(td, 1)
                with pe.Fori(0, NH // 2) as it:
                    def add(q):
                        u, j, i, c, m = chunks[q]
                        pe.wait_ge(tlr, it * NC + (q + 3))
                        if c == 0:
                            pe.wait_ge(oo, it * NU + (u + 1))
                        for b in range(m):
                            for part in (th, tl):
                                last = pe.matmul(o[:, u % 2, 0:P], part[:, q % TS, P * b:P * b + P], g.vd[:, c + b],
                                                 start=(c + b == 0 and part is th), stop=(c + b == i and part is tl))
                        last.then_inc(vd, 1)

                    for s in range(NU + 1):
                        if s < NU:
                            j, i = units[s]
                            w = P * (i + 1)
                            if i == NT - 1:
                                pe.wait_ge(loaded[j], it * 32 + 32)
                            pe.wait_ge(tt, it * NU + (s + 1))
                            qb = qs[:, j, P * i:P * i + P]
                            for c in range(0, w, HALF):
                                x = slice(c, min(c + HALF, w))
                                pe.matmul(z[:, s % 2, x], qb, g.kdh[:, x], start=True, stop=False)
                                last = pe.matmul(z[:, s % 2, x], qb, g.kdl[:, x], start=False, stop=True)
                            last.then_inc(zr, 1)
                        for q in of(s - 1):
                            u, j, i, c, m = chunks[q]
                            pe.wait_ge(ex, it * NU + (u + 3))
                            pe.wait_ge(tlr, it * NC + (q + 1))
                            for b in range(m):
                                last = pe.transpose(tr[:, q % 2, P * b:P * b + P],
                                                    pe_[:, u % 2, P * (c + b):P * (c + b) + P], g.ident[:])
                            last.then_inc(td, 1)
                            if q >= 1:
                                add(q - 1)
                    add(NC - 1)
                pe.wait_ge(tt, STEPS * NU + 2)
                pe.wait_ge(tlr, STEPS * NC + 2)
                pe.wait_ge(oo, STEPS * NU + 2)
                pe.wait_ge(accd, 6)
                for n in range(16):
                    m = pe.matmul(z[:, 0, n:n + 1], acc[:, 2 + n // 4, P * (n % 4):P * (n % 4) + P], g.ones[:, 0:1],
                                  start=(n == 0), stop=True, skip_group_check=True)
                m.then_inc(colm, 1)
                pe.wait_ge(accd, len(mods))
                for c, r, half, ps in rows:
                    if c == len(mods) - 1:
                        pe.wait_ge(mbs, 1)
                    pe.matmul(ps, g.ones[:, 0:1], acc[:, c], start=True, stop=True).then_inc(rowm, 1)


def phase4(nc, k, g, A, vecs):
    NF = 2 * KD
    with ExitStack() as ctx:
        wl = sbuf(nc, ctx, "wo_lo", [P, KD, D], F32R)
        wh = sbuf(nc, ctx, "wo_hi", [P, KD, D], F32R)
        oh = sbuf(nc, ctx, "oT_hi", [P, KD, SEQ], F32R)
        ol = sbuf(nc, ctx, "oT_lo", [P, KD, SEQ], F32R)
        g1 = sbuf(nc, ctx, "gate1", [P, D])
        sq = sbuf(nc, ctx, "o_sq", [P, 2, HALF])
        hf = sbuf(nc, ctx, "o_full", [P, 2, HALF])
        rb = sbuf(nc, ctx, "sb_rstd", [P, HALF])
        s4 = sbuf(nc, ctx, "sb_ss", [P, 4 * NT])
        rc = sbuf(nc, ctx, "sb_rstd_col", [P, NT])
        ss = sbuf(nc, ctx, "d_ss", [P, NT])
        ps_s = psum(nc, ctx, "ps_ss", [P, 2, HALF])
        ps_t = psum(nc, ctx, "ps_ot", [P, 2, HALF])
        ps_y = psum(nc, ctx, "ps_y", [P, 4, HALF])

        x_loaded = k.sems("x1_loaded", NT)
        wo_loaded = k.sems("wo_loaded", KD)
        g1_loaded = k.sem("gate1_loaded")
        whr = k.sem("wo_hi_ready")
        wlr = k.sem("wo_lo_ready")
        dss = k.sem("d_ss_ready")
        dsn = k.sem("d_ss_scaled")
        drs = k.sem("d_rstd_ready")
        dsc = k.sem("d_scaled")
        sqd = k.sem("o_sq_ready")
        sqm = k.sem("o_sq_summed")
        ssr = k.sem("sb_ss_ready")
        svr = k.sem("sb_var_ready")
        dgr = k.sem("diag_ready")
        spr = k.sem("rstd_spread")
        rbr = k.sem("sb_rstd_spread_ready")
        srs = k.sem("sb_rstd_ready")
        tr = k.sem("o_transposed")
        hfr = k.sem("o_full_ready")
        hfd = k.sem("o_full_ready_dsa")
        ohr = k.sem("oT_hi_ready")
        olr = k.sem("oT_lo_ready")
        ym = k.sem("y_summed")
        yg = k.sem("y_gated")
        x1r = k.sem("x1_ready")
        s2 = k.sem("ss2_ready")
        xb = A["x"][0].rearrange("(i p) d -> i p d", p=P)
        half = lambda h: slice(HALF * h, HALF * h + HALF)

        with nc.Block() as block:
            @block.sync
            def _(sp):
                for t in range(KD):
                    sp.dma_start(g.x1[:, t], A["w_o"][0][P * t:P * t + P, :]).then_inc(wo_loaded[t], 16)
                sp.dma_start(g1[:], vecs[0:1, :].partition_broadcast(P)).then_inc(g1_loaded, 16)
                for i in range(NT):
                    sp.wait_ge(wlr, i + 1)
                    sp.dma_start(g.x1[:, i], xb[i]).then_inc(x_loaded[i], 16)

            @block.scalar
            def _(act):
                def square_sb(n):
                    h, f = n // NPAIR, n % NPAIR
                    if n >= 2:
                        act.wait_ge(sqm, n - 1)
                    act.activation(sq[:, n % 2], g.osb[:, f, half(h)], ACT.Square).then_inc(sqd, 1)

                for i in range(NT):
                    if i >= 2:
                        act.wait_ge(dss, i - 1)
                    act.activation(hf[:, i % 2], g.otok[:, i], ACT.Square, accum_out=ss[:, i:i + 1]).then_inc(dss, 1)
                for n in range(4):
                    square_sb(n)
                for i in range(NT):
                    act.wait_ge(drs, 1)
                    act.activation(g.otok[:, i], g.otok[:, i], ACT.Copy, scale=ss[:, i:i + 1]).then_inc(dsc, 1)
                    if i >= 4:
                        square_sb(i)
                for h in range(2):
                    for f in range(4):
                        n = KD * h + 4 + f
                        act.wait_ge(tr, 4 * h + f + 1)
                        act.wait_ge(dss, NT)
                        act.wait_ge(olr, n - 1)
                        act.activation(hf[:, n % 2], ps_t[:, f % 2], ACT.Copy,
                                       scale=g.cols[:, R_DG + f:R_DG + f + 1]).then_inc(hfd, 1)
                    for t in range(4 * h, 4 * h + 4):
                        act.wait_ge(wo_loaded[t], 16)
                        act.activation(wh[:, t], g.x1[:, t], ACT.Copy).then_inc(whr, 1)
                for i in range(NT):
                    act.wait_ge(x1r, 2 * i + 2)
                    if i >= 1:
                        act.wait_ge(s2, i)
                    act.activation(g.otok[:, 0:2], g.x1[:, i].rearrange("p (a n) -> p a n", a=2), ACT.Square,
                                   accum_out=g.ss2[:, i:i + 1]).then_inc(s2, 1)

            @block.gpsimd
            def _(pool):
                pool.wait_ge(dss, NT)
                pool.tensor_scalar(ss[:], ss[:], 1.0 / (NH * HD), EPS, ALU.mult, ALU.add).then_inc(dsn, 1)
                pool.wait_ge(dsn, 1)
                pool.tensor_tensor(ss[:], ss[:], g.nhalf[:], ALU.pow).then_inc(drs, 1)
                pool.wait_ge(svr, 1)
                pool.tensor_tensor(rc[:], rc[:], g.nhalf[:], ALU.pow).then_inc(srs, 1)
                for t in range(KD):
                    pool.wait_ge(whr, t + 1)
                    pool.tensor_tensor(wl[:, t], g.x1[:, t], wh[:, t].bitcast(F32), ALU.subtract)\
                        .then_inc(wlr, 1)

            @block.tensor
            def _(pe):
                def sum_sb(n):
                    h, f = n // NPAIR, n % NPAIR
                    pe.wait_ge(sqd, n + 1)
                    for b in range(4):
                        m = pe.matmul(ps_s[:, 0, NT * f + 4 * h + b:NT * f + 4 * h + b + 1],
                                      sq[:, n % 2, P * b:P * b + P], g.ones[:, 0:1], start=(n == 0 and b == 0),
                                      stop=True, skip_group_check=True)
                    m.then_inc(sqm, 1)

                def spread(h):
                    for b in range(4):
                        pe.wait_ge(dgr, 4 * h + b + 1)
                        m = pe.matmul(ps_s[:, 1, P * b:P * b + P], g.ones[:], sq[:, b % 2, 0:P], start=(b == 0), stop=True,
                                      skip_group_check=True)
                        m.then_inc(spr, 1)

                def transposes(h):
                    pe.wait_ge(dsc, 4 * h + 4)
                    for f in range(4):
                        n = 4 * h + f
                        if n >= 2:
                            pe.wait_ge(hfd, n - 1)
                        for b in range(4):
                            m = pe.transpose(ps_t[:, f % 2, P * b:P * b + P], g.otok[:, 4 * h + b, P * f:P * f + P],
                                             g.ident[:])
                        m.then_inc(tr, 1)

                for n in range(2 * NPAIR):
                    sum_sb(n)
                for h in range(2):
                    if h == 1:
                        pe.wait_ge(rbr, 1)
                    spread(h)
                    transposes(h)
                pe.wait_ge(wlr, KD)
                for i in range(NT):
                    pe.wait_ge(olr, KD * (i // 4) + KD)
                    b = slice(P * i, P * i + P)
                    for c in range(2):
                        n = 2 * i + c
                        if n >= 4:
                            pe.wait_ge(yg, n - 3)
                        for t in range(KD):
                            for x, w in ((oh, wh), (oh, wl), (ol, wh)):
                                m = pe.matmul(ps_y[:, n % 4], x[:, t, b], w[:, t, half(c)],
                                              start=(t == 0 and x is oh and w is wh), stop=(t == KD - 1 and x is ol))
                        m.then_inc(ym, 1)

            @block.vector
            def _(dve):
                def split(n):
                    h, f = n // KD, n % KD
                    dve.wait_ge(hfr, n + 1)
                    dve.tensor_copy(oh[:, f, half(h)], hf[:, n % 2]).then_inc(ohr, 1)
                    dve.wait_ge(ohr, n + 1)
                    dve.tensor_tensor(ol[:, f, half(h)], hf[:, n % 2], oh[:, f, half(h)].bitcast(F32),
                                      ALU.subtract).then_inc(olr, 1)

                dve.wait_ge(sqm, 2 * NPAIR)
                dve.tensor_copy(s4[:], ps_s[:, 0, 0:4 * NT]).then_inc(ssr, 1)
                for n in range(3):
                    dve.wait_ge(ssr, n + 1)
                    dve.tensor_tensor(s4[:, 0:NT], s4[:, 0:NT], s4[:, NT * (n + 1):NT * (n + 2)], ALU.add).then_inc(ssr, 1)
                dve.wait_ge(ssr, 4)
                dve.tensor_scalar(rc[:], s4[:, 0:NT], 1.0 / (NH * HD), EPS, ALU.mult, ALU.add).then_inc(svr, 1)
                for h in range(2):
                    dve.wait_ge(srs, 1)
                    for b in range(4):
                        n = 4 * h + b
                        if n >= 2:
                            dve.wait_ge(spr, n - 1)
                        dve.tensor_scalar(sq[:, b % 2, 0:P], g.ident[:], rc[:, n:n + 1], None, ALU.mult).then_inc(dgr, 1)
                    dve.wait_ge(spr, 4 * h + 4)
                    if h == 1:
                        dve.wait_ge(olr, KD)
                    dve.tensor_copy(rb[:], ps_s[:, 1]).then_inc(rbr, 1)
                    dve.wait_ge(rbr, h + 1)
                    dve.wait_ge(dss, NT)
                    for f in range(NPAIR):
                        n = KD * h + f
                        if n >= 2:
                            dve.wait_ge(olr, n - 1)
                        dve.scalar_tensor_tensor(out=hf[:, n % 2], in0=g.osb[:, f, half(h)],
                                                 scalar=g.cols[:, R_SBG + f:R_SBG + f + 1], in1=rb[:],
                                                 op0=ALU.mult, op1=ALU.mult).then_inc(hfr, 1)
                        split(n)
                    for f in range(4):
                        dve.wait_ge(hfd, 4 * h + f + 1)
                        dve.sem_inc(hfr, 1)
                        split(KD * h + 4 + f)
                dve.wait_ge(g1_loaded, 16)
                for i in range(NT):
                    dve.wait_ge(x_loaded[i], 16)
                    for c in range(2):
                        n = 2 * i + c
                        dve.wait_ge(ym, n + 1)
                        if n == 0:
                            dve.wait_ge(olr, 2 * KD)
                        else:
                            dve.wait_ge(x1r, n)
                        dve.tensor_tensor(hf[:, n % 2], ps_y[:, n % 4], g1[:, half(c)], ALU.mult).then_inc(yg, 1)
                        dve.wait_ge(yg, n + 1)
                        dve.tensor_tensor(g.x1[:, i, half(c)], g.x1[:, i, half(c)], hf[:, n % 2], ALU.add)\
                           .then_inc(x1r, 1)


def phase5(nc, k, g, A, vecs, out):
    MC = 2
    NCH = NM // MC
    UN = 2 * MC
    half = lambda h: slice(HALF * h, HALF * h + HALF)
    with ExitStack() as ctx:
        hh = sbuf(nc, ctx, "h2T_hi", [P, KD, SEQ], F32R)
        hl = sbuf(nc, ctx, "h2T_lo", [P, KD, SEQ], F32R)
        g2 = sbuf(nc, ctx, "gate2", [P, D])
        wr = sbuf(nc, ctx, "wgu_raw", [P, MC, 2, KD, P])
        wh = sbuf(nc, ctx, "wgu_hi", [P, MC, 2, KD, P], F32R)
        wl = sbuf(nc, ctx, "wgu_lo", [P, MC, 2, KD, P], F32R)
        dr = sbuf(nc, ctx, "wd_raw", [P, MC, D])
        dh = sbuf(nc, ctx, "wd_hi", [P, MC, D], F32R)
        dl = sbuf(nc, ctx, "wd_lo", [P, MC, D], F32R)
        sg = sbuf(nc, ctx, "silu_gate", [P, 2, HALF])
        af = sbuf(nc, ctx, "act_full", [P, 2, HALF])
        ssv = sbuf(nc, ctx, "ssv2", [P, NT])
        rstd = sbuf(nc, ctx, "rstd2", [P, NT])
        ssf = sbuf(nc, ctx, "ssf", [P, NT])
        rf = sbuf(nc, ctx, "rstdf", [P, NT])
        with ExitStack() as c:
            xh = sbuf(nc, c, "xhat", [P, 4, D])
        with ExitStack() as c:
            ah = sbuf(nc, c, "act_hi", [P, MC, SEQ], F32R)
            al = sbuf(nc, c, "act_lo", [P, MC, SEQ], F32R)
        afin, bfin = (wr[:, 0, j].rearrange("p t n -> p (t n)") for j in range(2))
        ps_g = psum(nc, ctx, "ps_gate", [P, 2, HALF])
        ps_u = psum(nc, ctx, "ps_up", [P, 2, HALF])
        ps_d = psum(nc, ctx, "ps_down", [P, 4, HALF])

        g2_loaded = k.sem("gate2_loaded")
        wr_loaded = k.sems("wgu_loaded", MC)
        dr_loaded = k.sem("wd_loaded")
        ssn = k.sem("ss2_scaled")
        rs = k.sem("rstd2_ready")
        xhr = k.sem("xhat2_ready")
        tr = k.sem("x1_transposed")
        hfr = k.sem("h2_full_ready")
        hir = k.sem("h2_hi_ready")
        lor = k.sem("h2_lo_ready")
        gu = k.sem("gate_up_summed")
        whr = k.sem("wgu_hi_ready")
        wlr = k.sem("wgu_lo_ready")
        sil = k.sem("silu_ready")
        gat = k.sem("act_full_ready")
        ahr = k.sem("act_hi_ready")
        alr = k.sem("act_lo_ready")
        dsc = k.sem("wd_scaled")
        dhr = k.sem("wd_hi_ready")
        dlr = k.sem("wd_lo_ready")
        dm = k.sem("down_summed")
        add = k.sem("down_added")
        sf = k.sem("ssf_ready")
        sfn = k.sem("ssf_scaled")
        rfr = k.sem("rstdf_ready")
        ab_loaded = k.sem("final_vectors_loaded")
        om = k.sem("out_scaled")
        od = k.sem("out_ready_dve")
        op = k.sem("out_ready_pool")
        stored = k.sem("out_stored")
        ob = out[0].rearrange("(i p) d -> i p d", p=P)
        ND = 2 * NT

        with nc.Block() as block:
            @block.sync
            def _(sp):
                w = [A[n][0].rearrange("(t p) n -> p t n", p=P) for n in ("w_gate", "w_up")]
                wd = A["w_down"][0]

                def load_gu(it, m):
                    for j in range(2):
                        x = w[j][:, :, P * m:P * m + P] if it is None else w[j][:, :, bass.ds(it * (MC * P) + P * m, P)]
                        sp.dma_start(wr[:, m, j], x).then_inc(wr_loaded[m], 16)

                def load_d(it):
                    x = wd[0:MC * P, :] if it is None else wd[bass.ds(it * (MC * P), MC * P), :]
                    sp.dma_start(dr[:], x.rearrange("(m p) n -> p m n", p=P)).then_inc(dr_loaded, 16)

                for m in range(MC):
                    load_gu(None, m)
                sp.dma_start(g2[:], vecs[1:2, :].partition_broadcast(P)).then_inc(g2_loaded, 16)
                load_d(None)
                with sp.Fori(1, NCH) as it:
                    for m in range(MC):
                        sp.wait_ge(wlr, it * MC + (m + 1))
                        load_gu(it, m)
                    sp.wait_ge(dlr, it + 1)
                    load_d(it)
                sp.wait_ge(wlr, NCH * MC + 1)
                sp.dma_start(bfin, vecs[2:3, :].partition_broadcast(P)).then_inc(ab_loaded, 16)
                sp.dma_start(afin, vecs[3:4, :].partition_broadcast(P)).then_inc(ab_loaded, 16)
                for i in range(NT):
                    sp.wait_ge(op if i % 2 else od, i // 2 + 1)
                    sp.dma_start(ob[i], g.x1[:, i]).then_inc(stored, 16)
                sp.wait_ge(stored, 16 * NT)

            @block.scalar
            def _(act):
                act.wait_ge(rs, 1)
                for h in range(2):
                    for b in range(4):
                        i = 4 * h + b
                        if h == 1:
                            act.wait_ge(tr, KD)
                        act.activation(xh[:, b], g.x1[:, i], ACT.Copy, scale=rstd[:, i:i + 1]).then_inc(xhr, 1)
                    for t in range(KD):
                        n = KD * h + t
                        act.wait_ge(tr, n + 1)
                        if n >= 2:
                            act.wait_ge(lor, n - 1)
                        act.activation(sg[:, n % 2], ps_d[:, n % 4], ACT.Identity, bias=g.b2[:, t:t + 1],
                                       scale=g.a2[:, t:t + 1]).then_inc(hfr, 1)
                with act.Fori(0, NCH) as it:
                    for m in range(MC):
                        act.wait_ge(wr_loaded[m], it * 32 + 32)
                        act.wait_ge(gu, it * UN + (2 * m + 2))
                        act.activation(wh[:, m], wr[:, m], ACT.Copy).then_inc(whr, 1)
                    for u in range(UN):
                        act.wait_ge(gu, it * UN + (u + 1 + 4))
                        act.wait_ge(gat, it * UN + (u + 1))
                        act.activation(sg[:, u % 2], ps_g[:, u % 2], ACT.Silu).then_inc(sil, 1)
                        if u == 0:
                            act.wait_ge(dsc, it + 1)
                            act.wait_ge(dm, it * ND + ND)
                            act.activation(dh[:], dr[:], ACT.Copy).then_inc(dhr, 1)
                for i in range(NT):
                    act.wait_ge(add, (NCH - 1) * ND + 2 * i + 2 + 4)
                    if i >= 1:
                        act.wait_ge(sf, i)
                    act.activation(sg[:], g.x1[:, i].rearrange("p (a n) -> p a n", a=2), ACT.Square,
                                   accum_out=ssf[:, i:i + 1]).then_inc(sf, 1)

            @block.gpsimd
            def _(pool):
                pool.sem_inc(wlr, MC)
                pool.sem_inc(dlr, 1)
                pool.tensor_scalar(ssv[:], g.ss2[:], 1.0 / D, EPS, ALU.mult, ALU.add).then_inc(ssn, 1)
                pool.wait_ge(ssn, 1)
                pool.tensor_tensor(rstd[:], ssv[:], g.nhalf[:], ALU.pow).then_inc(rs, 1)
                with pool.Fori(0, NCH) as it:
                    for m in range(MC):
                        pool.wait_ge(whr, it * MC + (m + 1))
                        pool.tensor_tensor(wl[:, m], wr[:, m], wh[:, m].bitcast(F32), ALU.subtract).then_inc(wlr, 1)
                    pool.wait_ge(dhr, it + 1)
                    pool.tensor_tensor(dl[:], dr[:], dh[:].bitcast(F32), ALU.subtract).then_inc(dlr, 1)
                pool.wait_ge(ab_loaded, 32)
                for i in range(NT):
                    pool.wait_ge(sf, i + 1)
                    s = slice(i, i + 1)
                    pool.tensor_scalar(ssf[:, s], ssf[:, s], 1.0 / D, EPS, ALU.mult, ALU.add).then_inc(sfn, 1)
                    pool.wait_ge(sfn, i + 1)
                    pool.tensor_tensor(rf[:, s], ssf[:, s], g.nhalf[:, 0:1], ALU.pow).then_inc(rfr, 1)
                    if i % 2:
                        pool.wait_ge(om, i + 1)
                        pool.tensor_tensor(g.x1[:, i], g.x1[:, i], bfin, ALU.add).then_inc(op, 1)

            @block.tensor
            def _(pe):
                pe.sem_inc(gu, 4)
                pe.sem_inc(dm, ND)
                for n in range(2 * KD):
                    h, t = n // KD, n % KD
                    pe.wait_ge(xhr, 4 * h + 4)
                    if n >= 4:
                        pe.wait_ge(hfr, n - 3)
                    for b in range(4):
                        m = pe.transpose(ps_d[:, n % 4, P * b:P * b + P], xh[:, b, P * t:P * t + P], g.ident[:])
                    m.then_inc(tr, 1)
                pe.wait_ge(lor, 2 * KD)
                with pe.Fori(0, NCH) as it:
                    for m in range(MC):
                        pe.wait_ge(wlr, it * MC + (m + 1 + MC))
                        for h in range(2):
                            u = 2 * m + h
                            pe.wait_ge(gat, it * UN + (u + 1))
                            for j, ps in ((0, ps_g), (1, ps_u)):
                                for t in range(KD):
                                    for w, x in ((wh, hh), (wh, hl), (wl, hh)):
                                        last = pe.matmul(ps[:, u % 2], w[:, m, j, t], x[:, t, half(h)],
                                                         start=(t == 0 and w is wh and x is hh),
                                                         stop=(t == KD - 1 and w is wl))
                            last.then_inc(gu, 1)
                    pe.wait_ge(dlr, it + 2)
                    for n in range(ND):
                        i, c = n // 2, n % 2
                        if n % NT == 0:
                            pe.wait_ge(alr, it * UN + (3 + n // NT + 2))
                        pe.wait_ge(add, it * ND + (n + 1))
                        for m in range(MC):
                            for x, w in ((ah, dh), (ah, dl), (al, dh)):
                                last = pe.matmul(ps_d[:, n % 4], x[:, m, P * i:P * i + P], w[:, m, half(c)],
                                                 start=(m == 0 and x is ah and w is dh), stop=(m == MC - 1 and x is al))
                        last.then_inc(dm, 1)

            @block.vector
            def _(dve):
                dve.sem_inc(gat, 2)
                dve.sem_inc(alr, 2)
                dve.sem_inc(add, 4)
                for n in range(2 * KD):
                    h, t = n // KD, n % KD
                    dve.wait_ge(hfr, n + 1)
                    dve.tensor_copy(hh[:, t, half(h)], sg[:, n % 2]).then_inc(hir, 1)
                    dve.wait_ge(hir, n + 1)
                    dve.tensor_tensor(hl[:, t, half(h)], sg[:, n % 2], hh[:, t, half(h)].bitcast(F32),
                                      ALU.subtract).then_inc(lor, 1)
                dve.wait_ge(g2_loaded, 16)
                with dve.Fori(0, NCH) as it:
                    dve.wait_ge(dr_loaded, it * 16 + 16)
                    for m in range(MC):
                        ins = dve.tensor_tensor(dr[:, m], dr[:, m], g2[:], ALU.mult)
                    ins.then_inc(dsc, 1)
                    for u in range(UN):
                        m, h = u // 2, u % 2
                        dve.wait_ge(sil, it * UN + (u + 1))
                        dve.wait_ge(alr, it * UN + (u + 1))
                        dve.tensor_tensor(af[:, u % 2], sg[:, u % 2], ps_u[:, u % 2], ALU.mult).then_inc(gat, 1)
                        dve.wait_ge(gat, it * UN + (u + 1 + 2))
                        dve.wait_ge(dm, it * ND + (NT * h + NT))
                        dve.tensor_copy(ah[:, m, half(h)], af[:, u % 2]).then_inc(ahr, 1)
                        dve.wait_ge(ahr, it * UN + (u + 1))
                        dve.tensor_tensor(al[:, m, half(h)], af[:, u % 2], ah[:, m, half(h)].bitcast(F32),
                                          ALU.subtract).then_inc(alr, 1)
                    for n in range(ND):
                        i, c = n // 2, n % 2
                        dve.wait_ge(dm, it * ND + (n + 1 + ND))
                        dve.wait_ge(add, it * ND + (n + 1))
                        dve.tensor_tensor(g.x1[:, i, half(c)], ps_d[:, n % 4], g.x1[:, i, half(c)], ALU.add)\
                           .then_inc(add, 1)
                dve.wait_ge(ab_loaded, 32)
                for i in range(NT):
                    dve.wait_ge(rfr, i + 1)
                    dve.scalar_tensor_tensor(out=g.x1[:, i], in0=g.x1[:, i], scalar=rf[:, i:i + 1], in1=afin,
                                             op0=ALU.mult, op1=ALU.mult).then_inc(om, 1)
                    if i % 2 == 0:
                        dve.wait_ge(om, i + 1)
                        dve.tensor_tensor(g.x1[:, i], g.x1[:, i], bfin, ALU.add).then_inc(od, 1)


class Names:
    pass


def emit(nc, A, out, upto=9):
    with ExitStack() as ctx:
        k = Kit(nc)
        scr = nc.dram_tensor("scr_qkv", [16, 2, P, SEQ], F32, kind="Internal").ap()
        vecs = nc.dram_tensor("scr_vectors", [4, D], F32, kind="Internal").ap()
        g = Names()
        g.ident = sbuf(nc, ctx, "ident", [P, P])
        g.ones = sbuf(nc, ctx, "ones", [P, P])
        g.nhalf = sbuf(nc, ctx, "nhalf", [P, NT])
        g.cols = sbuf(nc, ctx, "cols", [P, P])
        g.csil = sbuf(nc, ctx, "csil", [P, KD])
        g.a2 = sbuf(nc, ctx, "a2", [P, KD])
        g.b2 = sbuf(nc, ctx, "b2", [P, KD])
        g.ss2 = sbuf(nc, ctx, "ss2", [P, NT])
        with ExitStack() as co:
            with ExitStack() as c03:
                g.bigid = sbuf(nc, c03, "big_ident", [P, P], F32R)
                g.tneg_f = sbuf(nc, c03, "tneg_f", [P, P])
                g.tneg = sbuf(nc, c03, "tneg", [P, P], F32R)
                g.nneg = sbuf(nc, c03, "nneg", [P, P], F32R)
                g.qscale = sbuf(nc, c03, "qscale", [P, 16])
                g.nslope = sbuf(nc, c03, "nslope", [P, NH])
                g.a1 = sbuf(nc, c03, "a1", [P, KD])
                g.b1 = sbuf(nc, c03, "b1", [P, KD])
                g.wtok = sbuf(nc, c03, "wtok", [P, NT, NIH])
                g.rkv = sbuf(nc, c03, "rkv", [P, NT])
                g.dist = sbuf(nc, c03, "dist", [P, SEQ])
                g.score = sbuf(nc, c03, "score", [P, soff(NT)])
                g.kdh = sbuf(nc, c03, "kdh", [P, SEQ], F32R)
                g.kdl = sbuf(nc, c03, "kdl", [P, SEQ], F32R)
                g.vd = sbuf(nc, c03, "vd", [P, NT, P], F32R)
                with ExitStack() as c01:
                    g.hTh = sbuf(nc, c01, "hTh", [P, KD, SEQ], F32R)
                    g.hTl = sbuf(nc, c01, "hTl", [P, KD, SEQ], F32R)
                    with ExitStack() as c0:
                        g.dist_i = sbuf(nc, c0, "dist_i", [P, SEQ], I32)
                        phase0(nc, k, g, A)
                    if upto >= 1:
                        phase1(nc, k, g, A, scr)
                k.release()
                g.osb = co.enter_context(nc.sbuf_tensor("o_sbT", [P, NPAIR, SEQ], F32, side="right"))
                g.otok = co.enter_context(nc.sbuf_tensor("o_dtok", [P, NT, NH * HD], F32, side="right"))
                if upto >= 2:
                    phase2(nc, k, g, scr)
                if upto >= 3:
                    phase3(nc, k, g, A, scr, vecs)
            k.release()
            g.x1 = sbuf(nc, ctx, "x1", [P, NT, D])
            if upto >= 4:
                phase4(nc, k, g, A, vecs)
        if upto >= 5:
            phase5(nc, k, g, A, vecs, out)
        k.release()


_INS = ["x", "c", "w_mod", "b_mod", "norm1_gain", "norm2_gain", "w_in", "kv_gain", "w_uk", "w_uv", "sb_out_gain",
        "dsa_out_gain", "w_o", "w_gate", "w_up", "w_down", "w_mod_final", "b_mod_final", "final_gain"]
_OUTS = [((1, SEQ, D), "float32")]


def kernel(**inputs):
    import numpy as _np
    import concourse.bacc as _bacc
    from concourse import mybir as _mybir
    from concourse.bass_utils import run_bass_kernel_spmd as _run

    nc = _bacc.Bacc("TRN2", target_bir_lowering=False, num_devices=1)
    arrays, args = {}, {}
    for name in _INS:
        a = _np.ascontiguousarray(inputs[name])
        arrays[f"in_{name}_dram"] = a
        args[name] = nc.dram_tensor(f"in_{name}_dram", a.shape, _mybir.dt.from_np(a.dtype), kind="ExternalInput").ap()
    out = nc.dram_tensor("out_0_dram", _OUTS[0][0], _mybir.dt.float32, kind="ExternalOutput").ap()
    emit(nc, args, out)
    r = _run(nc, [arrays], core_ids=[0])
    return r.results[0]["out_0_dram"]
```

```python
from contextlib import ExitStack

import concourse.bass as bass
from concourse import mybir

F32 = mybir.dt.float32
F32R = mybir.dt.float32r
I32 = mybir.dt.int32
ALU = mybir.AluOpType
ACT = mybir.ActivationFunctionType
AX = mybir.AxisListType

P = 128
SEQ = 1024
D = 1024
NT = SEQ // P
KD = D // P
HD = 64
NH = 8
NPAIR = NH // 2
KV = D // 4
NIH = 4
TOPK = 256
FF = 2816
NM = FF // P
EPS = 1e-6
BIG = 1e30
HALF = SEQ // 2
ZCLAMP = 40.0

C_SBQ, C_SBK, C_SBV, C_DQ, C_LAT = 0, 512, 1024, 1536, 2048
C_IQ = C_LAT + KV
C_IK = C_IQ + NIH * HD
IKW = HD + NIH

NACT = 3

R_BMOD, R_N1, R_N2, R_KV, R_SBG, R_DG, R_C = 0, 48, 56, 64, 66, 70, 74
NROWS = R_C + KD


def soff(i):
    return P * (i * (i + 1) // 2)


class Kit:

    def __init__(self, nc):
        self.nc, self.used = nc, []

    def sem(self, name):
        self.used.append(self.nc.alloc_semaphore(name=name))
        return self.used[-1]

    def release(self):
        self.nc.clear_and_free_semaphores(self.used)
        self.nc.all_engine_barrier()
        self.used = []

    def sems(self, name, n):
        return [self.sem(f"{name}{i}") for i in range(n)]


def sbuf(nc, ctx, name, shape, dt=F32):
    return ctx.enter_context(nc.sbuf_tensor(name, shape, dt))


def psum(nc, ctx, name, shape, dt=F32):
    return ctx.enter_context(nc.psum_tensor(name, shape, dt))


def phase0(nc, k, g, A):
    with ExitStack() as ctx:
        xt = sbuf(nc, ctx, "xt", [P, NT, D])
        wm = sbuf(nc, ctx, "wm", [P, 2, KD, 512])
        acc = sbuf(nc, ctx, "mod_acc", [P, 4, 512])
        vec = sbuf(nc, ctx, "vec", [P, P])
        junk = sbuf(nc, ctx, "sq_junk", [P, 2, D])
        ss = sbuf(nc, ctx, "ss1", [P, NT])
        ssv = sbuf(nc, ctx, "ssv1", [P, NT])
        rstd = sbuf(nc, ctx, "rstd1", [P, NT])
        mb = sbuf(nc, ctx, "mb1", [P, 16])
        hf = sbuf(nc, ctx, "hfull", [P, 2, HALF])
        ps_t = psum(nc, ctx, "ps_t0", [P, 4, HALF])
        ps_v = psum(nc, ctx, "ps_v0", [P, 512])
        ps_m = psum(nc, ctx, "ps_m0", [P, 512])

        vec_loaded = k.sem("vec_loaded")
        x_loaded = k.sems("x_loaded", NT)
        wm_loaded = k.sems("wm_loaded", 2)
        const0 = k.sem("const_zeroed")
        scales_set = k.sem("scales_set")
        const_ready = k.sem("const_ready")
        vecT = k.sem("vecT_done")
        cols_ready = k.sem("cols_ready")
        csil_ready = k.sem("csil_ready")
        chain = k.sem("mod_chain")
        accd = k.sem("mod_acc_done")
        modm = k.sem("mod_summed")
        mbs = k.sem("mod_biased")
        ab = k.sem("ab1_ready")
        ssd = k.sem("ss1_done")
        ssn = k.sem("ss1_scaled")
        rs = k.sem("rstd1_ready")
        xh = k.sem("xhat_ready")
        tr = k.sem("x_transposed")
        hfs = k.sem("hfull_ready")
        his = k.sem("hhi_ready")
        los = k.sem("hlo_ready")
        rows = [(A["b_mod"], R_BMOD, 48), (A["norm1_gain"], R_N1, KD), (A["norm2_gain"], R_N2, KD),
                (A["kv_gain"], R_KV, 2), (A["sb_out_gain"], R_SBG, 4), (A["dsa_out_gain"], R_DG, 4),
                (A["c"], R_C, KD)]
        w_mod = A["w_mod"][0].rearrange("(t p) n -> p t n", p=P)
        xb = A["x"][0].rearrange("(i p) d -> i p d", p=P)

        with nc.Block() as block:
            @block.sync
            def _(sp):
                for src, r, n in rows:
                    sp.dma_start(vec[r:r + n, :], src.rearrange("a (r p) -> (a r) p", p=P)).then_inc(vec_loaded, 16)
                for j in range(4):
                    if j >= 2:
                        for i in range(4 * j - 8, 4 * j - 4):
                            sp.dma_start(xt[:, i, :], xb[i]).then_inc(x_loaded[i], 16)
                        sp.wait_ge(accd, j - 1)
                    sp.dma_start(wm[:, j % 2], w_mod[:, :, 512 * j:512 * j + 512]).then_inc(wm_loaded[j % 2], 16)

            @block.gpsimd
            def _(pool):
                pool.memset(g.ident[:], 0.0).then_inc(const0, 1)
                pool.memset(g.ones[:], 1.0).then_inc(const0, 1)
                pool.memset(g.tneg_f[:], -1.0).then_inc(const0, 1)
                pool.memset(g.nhalf[:], -0.5).then_inc(const0, 1)
                pool.wait_ge(const0, 4)
                pool.affine_select(out=g.ident[:], in_=g.ident[:], compare_op=ALU.not_equal, fill=1.0,
                                   base=0, pattern=[[-1, P]], channel_multiplier=1).then_inc(const_ready, 1)
                pool.affine_select(out=g.tneg_f[:], in_=g.tneg_f[:], compare_op=ALU.is_ge, fill=0.0,
                                   base=0, pattern=[[-1, P]], channel_multiplier=1).then_inc(const_ready, 1)
                pool.iota(g.dist_i[:], pattern=[[1, SEQ]], base=-(SEQ - P), channel_multiplier=-1).then_inc(const_ready, 1)
                pool.wait_ge(const_ready, 3)
                pool.tensor_copy(g.tneg[:], g.tneg_f[:]).then_inc(const_ready, 1)
                pool.tensor_copy(g.dist[:], g.dist_i[:]).then_inc(const_ready, 1)
                pool.tensor_scalar(g.bigid[:], g.ident[:], BIG, None, ALU.mult).then_inc(const_ready, 1)
                pool.tensor_scalar(g.nneg[:], g.ones[:], -1.0, None, ALU.mult).then_inc(const_ready, 1)
                for j in range(2):
                    pool.wait_ge(ssd, 4 * j + 4)
                    s = slice(4 * j, 4 * j + 4)
                    pool.tensor_scalar(ssv[:, s], ss[:, s], 1.0 / D, EPS, ALU.mult, ALU.add).then_inc(ssn, 1)
                    pool.wait_ge(ssn, j + 1)
                    pool.tensor_tensor(rstd[:, s], ssv[:, s], g.nhalf[:, s], ALU.pow).then_inc(rs, 1)

            @block.scalar
            def _(act):
                act.wait_ge(cols_ready, 1)
                act.activation(g.csil[:], g.cols[:, R_C:R_C + KD], ACT.Silu).then_inc(csil_ready, 1)

                def square(i):
                    act.wait_ge(x_loaded[i], 16)
                    if i >= 2:
                        act.wait_ge(ssd, i - 1)
                    act.activation(junk[:, i % 2], xt[:, i, :], ACT.Square, accum_out=ss[:, i:i + 1]).then_inc(ssd, 1)

                def normalise(i):
                    act.wait_ge(rs, i // 4 + 1)
                    act.activation(xt[:, i, :], xt[:, i, :], ACT.Copy, scale=rstd[:, i:i + 1]).then_inc(xh, 1)

                def modulate(n):
                    t = n % KD
                    act.wait_ge(tr, n + 1)
                    act.wait_ge(ab, 2)
                    if n >= 2:
                        act.wait_ge(los, n - 1)
                    act.activation(hf[:, n % 2], ps_t[:, n % 4], ACT.Identity,
                                   bias=g.b1[:, t:t + 1], scale=g.a1[:, t:t + 1]).then_inc(hfs, 1)

                for i in range(4):
                    square(i)
                for i in range(4):
                    normalise(i)
                for i in range(4, NT):
                    square(i)
                for i in range(4, NT):
                    normalise(i)
                for n in range(2 * KD):
                    modulate(n)

            @block.tensor
            def _(pe):
                pe.wait_ge(const_ready, 2)
                pe.wait_ge(vec_loaded, 16 * len(rows))
                pe.transpose(ps_v[:, 0:NROWS], vec[0:NROWS, :], g.ident[0:NROWS, 0:NROWS]).then_inc(vecT, 1)

                def transposes(n):
                    half, t = n // KD, n % KD
                    pe.wait_ge(xh, 4 * half + 4)
                    if n >= 4:
                        pe.wait_ge(hfs, n - 3)
                    for i in range(4):
                        m = pe.transpose(ps_t[:, n % 4, P * i:P * i + P],
                                         xt[:, 4 * half + i, P * t:P * t + P], g.ident[:])
                    m.then_inc(tr, 1)

                for n in range(4):
                    transposes(n)
                for j in range(4):
                    pe.wait_ge(accd, j + 1)
                    for t in range(4):
                        m = pe.matmul(ps_m[:, 4 * j + t:4 * j + t + 1], acc[:, j, P * t:P * t + P],
                                      g.ones[:, 0:1], start=(j == 0 and t == 0), stop=True,
                                      skip_group_check=True)
                    m.then_inc(modm, 1)
                for n in range(4, 2 * KD):
                    transposes(n)

            @block.vector
            def _(dve):
                for h in range(NH):
                    dve.memset(g.qscale[HD * (h % 2):HD * (h % 2) + HD, 12 + h // 2:13 + h // 2],
                                0.125 * 2.0 ** (h + 1)).then_inc(scales_set, 1)
                    dve.memset(g.nslope[:, h:h + 1], -(2.0 ** -(h + 1))).then_inc(scales_set, 1)
                dve.memset(g.qscale[:, 0:4], 0.125).then_inc(scales_set, 1)
                dve.memset(g.qscale[:, 4:12], 1.0).then_inc(scales_set, 1)
                dve.wait_ge(vecT, 1)
                dve.tensor_copy(g.cols[:, 0:NROWS], ps_v[:, 0:NROWS]).then_inc(cols_ready, 1)
                dve.wait_ge(csil_ready, 1)
                for j in range(4):
                    dve.wait_ge(wm_loaded[j % 2], 16 * (j // 2 + 1))
                    dve.tensor_scalar(acc[:, j], wm[:, j % 2, 0], g.csil[:, 0:1], None, ALU.mult).then_inc(chain, 1)
                    for t in range(1, KD):
                        dve.wait_ge(chain, 7 * j + t)
                        dve.scalar_tensor_tensor(out=acc[:, j], in0=wm[:, j % 2, t], scalar=g.csil[:, t:t + 1],
                                                 in1=acc[:, j], op0=ALU.mult, op1=ALU.add)\
                           .then_inc(chain if t < KD - 1 else accd, 1)
                dve.wait_ge(modm, 4)
                dve.tensor_tensor(mb[:], ps_m[:, 0:16], g.cols[:, 0:16], ALU.add).then_inc(mbs, 1)
                dve.wait_ge(mbs, 1)
                dve.tensor_copy(g.b1[:], mb[:, 0:8]).then_inc(ab, 1)
                dve.scalar_tensor_tensor(out=g.a1[:], in0=mb[:, 8:16], scalar=1.0, in1=g.cols[:, R_N1:R_N1 + 8],
                                         op0=ALU.add, op1=ALU.mult).then_inc(ab, 1)
                for n in range(2 * KD):
                    half, t = n // KD, n % KD
                    s = slice(HALF * half, HALF * half + HALF)
                    dve.wait_ge(hfs, n + 1)
                    dve.tensor_copy(g.hTh[:, t, s], hf[:, n % 2]).then_inc(his, 1)
                    dve.wait_ge(his, n + 1)
                    dve.tensor_tensor(g.hTl[:, t, s], hf[:, n % 2], g.hTh[:, t, s].bitcast(F32),
                                      ALU.subtract).then_inc(los, 1)


def tile_products(pe, ps, wh, wl, xh, xl, halves=2):
    for t in range(KD):
        for w, x in ((wh, xh), (wh, xl), (wl, xh)):
            for f in range(halves):
                s = slice(HALF * f, HALF * f + HALF)
                last = pe.matmul(ps[:, s], w[:, t, :], x[:, t, s], start=(t == 0 and w is wh and x is xh),
                                 stop=(t == KD - 1 and w is wl))
    return last


def phase1(nc, k, g, A, scr):
    with ExitStack() as ctx:
        raw = sbuf(nc, ctx, "win_raw", [P, 2, KD, P])
        wh = sbuf(nc, ctx, "win_hi", [P, 2, KD, P], F32R)
        wl = sbuf(nc, ctx, "win_lo", [P, 2, KD, P], F32R)
        evf = sbuf(nc, ctx, "proj_full", [P, 2, SEQ])
        evh = sbuf(nc, ctx, "proj_hi", [P, 2, SEQ], F32R)
        evl = sbuf(nc, ctx, "proj_lo", [P, 2, SEQ], F32R)
        rl = sbuf(nc, ctx, "relu", [P, 2, SEQ])
        junk = sbuf(nc, ctx, "cmp_junk", [P, soff(NT)], mybir.dt.uint8)
        lath = sbuf(nc, ctx, "lat_hi", [P, 2, SEQ], F32R)
        latl = sbuf(nc, ctx, "lat_lo", [P, 2, SEQ], F32R)
        wkr = sbuf(nc, ctx, "wukv_raw", [P, 2, P])
        wks = sbuf(nc, ctx, "wukv", [P, 2, P])
        wkh = sbuf(nc, ctx, "wukv_hi", [P, 2, P], F32R)
        wkl = sbuf(nc, ctx, "wukv_lo", [P, 2, P], F32R)
        ssv = sbuf(nc, ctx, "kv_ssv", [P, NT])
        cnt = sbuf(nc, ctx, "cnt", [P, 8])
        need = sbuf(nc, ctx, "need", [P, 8])
        key = sbuf(nc, ctx, "key", [P, 8], I32)
        bit = sbuf(nc, ctx, "bit", [P, 8], I32)
        cand = sbuf(nc, ctx, "cand", [P, 8], I32)
        sg = sbuf(nc, ctx, "sg", [P, 8], I32)
        thr = sbuf(nc, ctx, "thr", [P, 8], I32)
        keep = sbuf(nc, ctx, "keep", [P, 8])
        kbit = sbuf(nc, ctx, "kept_bit", [P, 8], I32)
        half16 = sbuf(nc, ctx, "key_halves", [P, 3, 8], I32)
        lim = sbuf(nc, ctx, "cnt_limit", [P, 8])
        with ExitStack() as c:
            qis = sbuf(nc, c, "qidx_stack", [P, NIH, SEQ], F32R)
            kih = sbuf(nc, c, "kidx_hi2", [P, SEQ], F32R)
            kil = sbuf(nc, c, "kidx_lo2", [P, SEQ], F32R)
        with ExitStack() as c:
            le = sbuf(nc, c, "below", [P, SEQ])
            eq = sbuf(nc, c, "eq", [P, SEQ])
            cum = sbuf(nc, c, "cum", [P, SEQ])
        ps_p = psum(nc, ctx, "ps_proj", [P, 2, SEQ])
        ps_s = psum(nc, ctx, "ps_score", [P, 2, SEQ])

        raw_loaded = k.sems("win_loaded", 2)
        whi = k.sem("win_hi_ready")
        wlo = k.sem("win_lo_ready")
        proj = k.sem("proj_done")
        full = k.sem("proj_full_ready")
        hi = k.sem("proj_hi_ready")
        lo = k.sem("proj_lo_ready")
        spill = k.sems("proj_spilled", 2)
        wtr = k.sem("idxw_transposed")
        wtk = k.sem("idxw_ready")
        sqr = k.sem("lat_squared")
        zs = k.sem("idx_logits")
        rel = k.sem("idx_relu")
        scd = k.sem("score_summed")
        dgm = k.sem("diag_masked")
        kvw = k.sem("wukv_loaded")
        kvs = k.sem("wukv_scaled")
        kvh = k.sem("wukv_hi_ready")
        kvl = k.sem("wukv_lo_ready")
        ssm = k.sem("lat_ss_summed")
        ssn = k.sem("lat_ss_scaled")
        rkv = k.sem("lat_rstd_ready")
        kvp = k.sem("kv_projected")
        kvt = k.sem("kv_tok_ready")
        vdh = k.sem("vd_hi_ready")
        vdl = k.sem("vd_lo_ready")
        ktr = k.sem("kd_transposed")
        kfl = k.sem("kd_full_ready")
        kdh = k.sem("kd_hi_ready")
        kdl = k.sem("kd_lo_ready")
        kdup = k.sem("kd_doubled")
        cb = k.sem("signs_summed")
        lims = k.sem("limits_set")
        tk = k.sem("topk_chain")
        sl = k.sem("select_chain")
        m01 = k.sem("first_blocks")

        w_in = A["w_in"][0].rearrange("(t p) n -> p t n", p=P)
        fixed = (C_IQ, C_IQ + P, C_IK, C_LAT, C_LAT + P)
        T_IKW, T_LAT, N1, NL = 2, 3, 5, 16
        units = [(i, h) for i in range(2, NT) for h in range(NIH)]
        base_spill = (128, 64)
        width = lambda n: IKW if n == T_IKW else P

        with nc.Block() as block:
            @block.sync
            def _(sp):
                def load(i, n):
                    if n >= 2:
                        sp.wait_ge(wlo, i + (n - 1))
                    c = fixed[n] if n < N1 else P * (n - N1)
                    src = w_in[:, :, bass.ds(i * P + c, P)] if n >= N1 else w_in[:, :, c:c + width(n)]
                    sp.dma_start(raw[:, n % 2, :, 0:width(n)], src).then_inc(raw_loaded[n % 2], 16)

                def stack_q(n):
                    for part, ready, top in ((evh, hi, 0), (evl, lo, HD)):
                        sp.wait_ge(ready, n + 1)
                        for j in range(2):
                            sp.dma_start(qis[top:top + HD, 2 * n + j, :].bitcast(F32),
                                         part[HD * j:HD * j + HD, n % 2].bitcast(F32)).then_inc(spill[n % 2], 16)

                def double_k():
                    for part, ready, dst in ((evh, hi, kih), (evl, lo, kil)):
                        sp.wait_ge(ready, T_IKW + 1)
                        for top in (0, HD):
                            sp.dma_start(dst[top:top + HD].bitcast(F32), part[0:HD, 0].bitcast(F32)).then_inc(spill[0], 16)

                def store(i, n):
                    for x, (part, ready) in enumerate(((evh, hi), (evl, lo))):
                        sp.wait_ge(ready, i + (n + 1))
                        sp.dma_start(scr[bass.ds(i + (n - N1), 1), x].rearrange("a p n -> (a p) n"),
                                     part[:, n % 2].bitcast(F32)).then_inc(spill[n % 2], 16)

                load(0, 0)
                load(0, 1)
                sp.dma_start(wkr[:, :, 0:HD], A["w_uk"][0].rearrange("(t p) n -> p t n", p=P)).then_inc(kvw, 16)
                sp.dma_start(wkr[:, :, HD:P], A["w_uv"][0].rearrange("(t p) n -> p t n", p=P)).then_inc(kvw, 16)
                load(0, 2)
                stack_q(0)
                load(0, 3)
                stack_q(1)
                load(0, 4)
                double_k()
                load(0, 5)
                load(0, 6)
                with sp.Fori(0, NL - 2, 2) as i:
                    for j in range(2):
                        load(i, N1 + 2 + j)
                        store(i, N1 + j)
                for j in range(2):
                    store(NL - 2, N1 + j)
                sp.wait_ge(kdl, 1)
                sp.dma_start(g.kdl[HD:P].bitcast(F32), g.kdl[0:HD].bitcast(F32)).then_inc(kdup, 16)
                sp.wait_ge(kdup, 16)
                for s in range(2):
                    sp.wait_ge(spill[s], base_spill[s] + 16 * NL)

            @block.scalar
            def _(act):
                def w_hi(i, n):
                    w = width(n)
                    act.wait_ge(raw_loaded[n % 2], i * 8 + 16 * (n // 2 + 1))
                    if n >= 2:
                        act.wait_ge(proj, i + (n - 1))
                    act.activation(wh[:, n % 2, :, 0:w], raw[:, n % 2, :, 0:w], ACT.Copy).then_inc(whi, 1)

                def evac(i, n, scale):
                    m = width(n)
                    act.wait_ge(proj, i + (n + 1))
                    if n >= 2:
                        act.wait_ge(lo, i + (n - 1))
                    act.activation(evf[0:m, n % 2], ps_p[0:m, n % 2], ACT.Copy, scale=scale).then_inc(full, 1)

                def e_hi(i, n, dst=None, spills=0):
                    m = width(n)
                    act.wait_ge(full, i + (n + 1))
                    if n >= N1 or spills:
                        act.wait_ge(spill[n % 2], i * 16 + spills)
                    act.activation(evh[0:m, n % 2] if dst is None else dst, evf[0:m, n % 2], ACT.Copy).then_inc(hi, 1)

                w_hi(0, 0)
                w_hi(0, 1)
                for n in range(3):
                    w_hi(0, n + 2)
                    evac(0, n, 0.125 if n < 2 else 1.0)
                    e_hi(0, n, spills=64 * (n == 2))
                act.wait_ge(wtr, 1)
                act.activation(g.wtok[:], ps_s[:, 0, 0:NIH * NT].rearrange("p (a b) -> p a b", b=NIH),
                               ACT.Copy, scale=0.5).then_inc(wtk, 1)
                act.wait_ge(kvw, 32)
                for t in range(2):
                    act.activation(wks[:, t], wkr[:, t], ACT.Copy, scale=g.cols[:, R_KV + t:R_KV + t + 1]).then_inc(kvs, 1)
                act.wait_ge(kvs, 2)
                act.activation(wkh[:], wks[:], ACT.Copy).then_inc(kvh, 1)
                w_hi(0, 5)
                evac(0, T_LAT, 1.0)
                e_hi(0, T_LAT, dst=lath[:, 0])
                for u, (i, h) in enumerate(units):
                    w = P * (i + 1)
                    act.wait_ge(zs, u + 1)
                    if u >= 2:
                        act.wait_ge(scd, u - 1)
                    act.activation(rl[:, u % 2, 0:w], ps_s[:, u % 2, 0:w], ACT.Relu).then_inc(rel, 1)
                def step(i, j):
                    evac(i, N1 + j, g.qscale[:, bass.ds(i + j, 1)])
                    e_hi(i, N1 + j, spills=base_spill[(N1 + j) % 2])

                def count(first):
                    act.wait_ge(tk, first + 6)
                    for c in range(NACT):
                        w = slice(soff(c + 2), soff(c + 3))
                        last = act.activation(junk[:, w].bitcast(mybir.dt.int8), g.score[:, w], ACT.Sign, scale=-1.0,
                                              bias=thr[:, c:c + 1].bitcast(F32), accum_out=cnt[:, c:c + 1])
                    last.then_inc(cb, 1)

                BT = (3, 2)
                CT = 31 // sum(BT) * 2
                evac(0, T_LAT + 1, 1.0)
                e_hi(0, T_LAT + 1, dst=lath[:, 1])
                w_hi(0, N1 + 1)
                for t in range(2):
                    act.wait_ge(scd, len(units) - 1 + t)
                    act.activation(rl[:, t], evf[:, (T_LAT + t) % 2], ACT.Square).then_inc(sqr, 1)
                for b in range(BT[0]):
                    count(8 * b)
                w_hi(0, N1 + 2)
                step(0, 0)
                act.wait_ge(ssm, 1)
                act.activation(ssv[:], ps_s[:, 0, 0:NT], ACT.Copy, scale=1.0 / KV).then_inc(ssn, 1)
                for b in range(BT[0], sum(BT)):
                    count(8 * b)
                act.wait_ge(kvp, 1)
                act.wait_ge(rkv, 1)
                for i in range(NT):
                    act.activation(rl[:, 0, P * i:P * i + P], ps_s[:, 1, P * i:P * i + P], ACT.Copy,
                                   scale=g.rkv[:, i:i + 1]).then_inc(kvt, 1)
                act.wait_ge(kvt, NT)
                act.activation(g.vd[:, :, 0:HD], rl[:, 0].rearrange("p (b d) -> p b d", b=NT)[:, :, HD:P],
                               ACT.Copy).then_inc(vdh, 1)
                w_hi(0, N1 + 3)
                step(0, 1)
                act.wait_ge(ktr, 1)
                act.activation(rl[0:HD, 1], ps_s[0:HD, 0], ACT.Copy).then_inc(kfl, 1)
                for top in (0, HD):
                    act.activation(g.kdh[top:top + HD], ps_s[0:HD, 0], ACT.Copy).then_inc(kdh, 1)
                with act.Fori(2, CT, 2) as i:
                    for j in range(2):
                        for b in range(BT[j]):
                            count(i * (sum(BT) * 4) + (BT[0] * j + b) * 8)
                        w_hi(i, N1 + 2 + j)
                        step(i, j)
                for b in range(sum(BT) * CT // 2, 31):
                    count(8 * b)
                with act.Fori(CT, NL - 2, 2) as i:
                    for j in range(2):
                        w_hi(i, N1 + 2 + j)
                        step(i, j)
                for j in range(2):
                    step(NL - 2, j)

            @block.gpsimd
            def _(pool):
                def w_lo(i, n):
                    w = width(n)
                    pool.wait_ge(whi, i + (n + 1))
                    if n >= 2:
                        pool.wait_ge(proj, i + (n - 1))
                    pool.tensor_tensor(wl[:, n % 2, :, 0:w], raw[:, n % 2, :, 0:w],
                                       wh[:, n % 2, :, 0:w].bitcast(F32), ALU.subtract).then_inc(wlo, 1)

                def e_lo(i, n, dst=None, high=None, spills=0):
                    m = width(n)
                    pool.wait_ge(hi, i + (n + 1))
                    if n >= N1 or spills:
                        pool.wait_ge(spill[n % 2], i * 16 + spills)
                    pool.tensor_tensor(evl[0:m, n % 2] if dst is None else dst, evf[0:m, n % 2],
                                       (evh[0:m, n % 2] if high is None else high).bitcast(F32),
                                       ALU.subtract).then_inc(lo, 1)

                w_lo(0, 0)
                w_lo(0, 1)
                for n in range(3):
                    w_lo(0, n + 2)
                    e_lo(0, n, spills=64 * (n == 2))
                pool.wait_ge(kvh, 1)
                pool.tensor_tensor(wkl[:], wks[:], wkh[:].bitcast(F32), ALU.subtract).then_inc(kvl, 1)
                w_lo(0, 5)
                e_lo(0, T_LAT, dst=latl[:, 0], high=lath[:, 0])
                for i in range(2):
                    s = g.score[:, soff(i):soff(i + 1)]
                    pool.tensor_copy(s, g.dist[:, SEQ - P * (i + 1):SEQ]).then_inc(m01, 1)
                for i in range(NT):
                    if i < 2:
                        pool.wait_ge(m01, i + 1)
                    else:
                        pool.wait_ge(scd, NIH * (i - 1))
                    s = g.score[:, soff(i + 1) - P:soff(i + 1)]
                    pool.affine_select(out=s, in_=s, compare_op=ALU.is_ge, fill=-BIG if i < 2 else -3e38,
                                       base=0, pattern=[[-1, P]], channel_multiplier=1).then_inc(dgm, 1)
                w_lo(0, N1 + 1)
                e_lo(0, T_LAT + 1, dst=latl[:, 1], high=lath[:, 1])
                w_lo(0, N1 + 2)
                e_lo(0, N1, spills=base_spill[N1 % 2])
                pool.wait_ge(ssn, 1)
                pool.tensor_scalar(ssv[:], ssv[:], 1.0, EPS, ALU.mult, ALU.add).then_inc(ssn, 1)
                pool.wait_ge(ssn, 2)
                pool.tensor_tensor(g.rkv[:], ssv[:], g.nhalf[:], ALU.pow).then_inc(rkv, 1)
                pool.wait_ge(vdh, 1)
                pool.tensor_tensor(g.vd[:, :, HD:P], rl[:, 0].rearrange("p (b d) -> p b d", b=NT)[:, :, HD:P],
                                   g.vd[:, :, 0:HD].bitcast(F32), ALU.subtract).then_inc(vdl, 1)
                w_lo(0, N1 + 3)
                e_lo(0, N1 + 1, spills=base_spill[(N1 + 1) % 2])
                pool.wait_ge(kfl, 1)
                pool.wait_ge(kdh, 1)
                pool.tensor_tensor(g.kdl[0:HD], rl[0:HD, 1], g.kdh[0:HD].bitcast(F32), ALU.subtract).then_inc(kdl, 1)
                with pool.Fori(2, NL - 2, 2) as i:
                    for j in range(2):
                        w_lo(i, N1 + 2 + j)
                        e_lo(i, N1 + j, spills=base_spill[(N1 + j) % 2])
                for j in range(2):
                    e_lo(NL - 2, N1 + j, spills=base_spill[(N1 + j) % 2])

            @block.tensor
            def _(pe):
                def project(i, n):
                    pe.wait_ge(wlo, i + (n + 1))
                    if n >= 2:
                        pe.wait_ge(full, i + (n - 1))
                    s, m = n % 2, width(n)
                    tile_products(pe, ps_p[0:m, s], wh[:, s, :, 0:m], wl[:, s, :, 0:m], g.hTh, g.hTl).then_inc(proj, 1)

                for n in range(3):
                    project(0, n)
                pe.wait_ge(full, T_IKW + 1)
                for i in range(NT):
                    last = pe.transpose(ps_s[:, 0, NIH * i:NIH * i + NIH], evf[HD:IKW, 0, P * i:P * i + P],
                                        g.ident[HD:IKW, HD:IKW])
                last.then_inc(wtr, 1)
                project(0, T_LAT)
                pe.wait_ge(wtk, 1)
                pe.wait_ge(spill[0], 128)
                pe.wait_ge(spill[1], 64)
                for u, (i, h) in enumerate(units):
                    if u >= 2:
                        pe.wait_ge(rel, u - 1)
                    w = P * (i + 1)
                    for c in range(0, w, HALF):
                        s = slice(c, min(c + HALF, w))
                        q = qis[:, h, P * i:P * i + P]
                        pe.matmul(ps_s[:, u % 2, s], q, kih[:, s], start=True, stop=False)
                        last = pe.matmul(ps_s[:, u % 2, s], q, kil[:, s], start=False, stop=True)
                    last.then_inc(zs, 1)
                project(0, T_LAT + 1)
                project(0, N1)
                pe.wait_ge(sqr, 2)
                pe.wait_ge(rel, len(units))
                for i in range(NT):
                    for t in range(2):
                        last = pe.matmul(ps_s[:, 0, i:i + 1], rl[:, t, P * i:P * i + P], g.ones[:, 0:1],
                                         start=(t == 0), stop=(t == 1))
                last.then_inc(ssm, 1)
                pe.wait_ge(kvl, 1)
                pe.wait_ge(lo, T_LAT + 2)
                for i in range(NT):
                    for t in range(2):
                        for x, w in ((lath, wkh), (lath, wkl), (latl, wkh)):
                            last = pe.matmul(ps_s[:, 1, P * i:P * i + P], x[:, t, P * i:P * i + P], w[:, t],
                                             start=(t == 0 and x is lath and w is wkh), stop=(t == 1 and x is latl))
                last.then_inc(kvp, 1)
                project(0, N1 + 1)
                pe.wait_ge(kvt, NT)
                for i in range(NT):
                    last = pe.transpose(ps_s[:, 0, P * i:P * i + P], rl[:, 0, P * i:P * i + P], g.ident[:])
                last.then_inc(ktr, 1)
                with pe.Fori(2, NL, 2) as i:
                    for j in range(2):
                        project(i, N1 + j)

            @block.vector
            def _(dve):
                for u, (i, h) in enumerate(units):
                    w = P * (i + 1)
                    s = g.score[:, soff(i):soff(i + 1)]
                    dve.wait_ge(rel, u + 1)
                    if h == 0:
                        dve.tensor_scalar(s, rl[:, u % 2, 0:w], g.wtok[:, i, 0:1], None, ALU.mult).then_inc(scd, 1)
                    else:
                        dve.wait_ge(scd, u)
                        dve.scalar_tensor_tensor(out=s, in0=rl[:, u % 2, 0:w], scalar=g.wtok[:, i, h:h + 1], in1=s,
                                                 op0=ALU.mult, op1=ALU.add).then_inc(scd, 1)
                dve.memset(bit[:], 1 << 30).then_inc(tk, 1)
                dve.wait_ge(dgm, NT)

                def counts(at, done, op=ALU.is_ge, cols=range(NT - 2)):
                    for i in (c + 2 for c in cols):
                        w = slice(soff(i), soff(i + 1))
                        last = dve.tensor_scalar(junk[:, w], g.score[:, w], at(i - 2), None, op, ALU.add,
                                                 accum_out=cnt[:, i - 2:i - 1])
                    last.then_inc(done, 1)

                NB = NT - 2
                b = slice(0, NB)
                for c in range(NB):
                    n = P * (c + 3)
                    dve.memset(lim[:, c:c + 1], float(n - 2 * TOPK if c < NACT else n - TOPK)).then_inc(lims, 1)
                counts(lambda i: 0.0, tk)
                dve.wait_ge(tk, 2)
                dve.wait_ge(lims, NB)
                dve.tensor_scalar(key[:, b], cnt[:, b], float(TOPK), -2.0 ** 31, ALU.is_lt, ALU.mult).then_inc(tk, 1)

                with dve.Fori(0, 31) as n:
                    dve.wait_ge(tk, n * 8 + 3)
                    dve.tensor_tensor(cand[:, b], key[:, b], bit[:, b], ALU.bitwise_or).then_inc(tk, 1)
                    dve.wait_ge(tk, n * 8 + 4)
                    dve.tensor_scalar(sg[:, b], cand[:, b], 31, 0x7FFFFFFF, ALU.arith_shift_right,
                                      ALU.bitwise_and).then_inc(tk, 1)
                    dve.wait_ge(tk, n * 8 + 5)
                    dve.tensor_tensor(thr[:, b], cand[:, b], sg[:, b], ALU.bitwise_xor).then_inc(tk, 1)
                    dve.wait_ge(tk, n * 8 + 6)
                    counts(lambda i: thr[:, i:i + 1].bitcast(F32), tk, ALU.is_lt, range(NACT, NB))
                    dve.wait_ge(tk, n * 8 + 7)
                    dve.wait_ge(cb, n + 1)
                    dve.tensor_tensor(keep[:, b], cnt[:, b], lim[:, b], ALU.is_le).then_inc(tk, 1)
                    dve.wait_ge(tk, n * 8 + 8)
                    dve.tensor_tensor(kbit[:, b], keep[:, b], bit[:, b], ALU.mult).then_inc(tk, 1)
                    dve.wait_ge(tk, n * 8 + 9)
                    dve.tensor_tensor(key[:, b], key[:, b], kbit[:, b], ALU.bitwise_or).then_inc(tk, 1)
                    dve.tensor_scalar(bit[:, b], bit[:, b], 1, None, ALU.logical_shift_right).then_inc(tk, 1)
                dve.wait_ge(tk, 31 * 8 + 3)
                done = [0]

                def then(ins):
                    ins.then_inc(sl, 1)
                    done[0] += 1
                    dve.wait_ge(sl, done[0])

                def threshold():
                    then(dve.tensor_scalar(sg[:, b], key[:, b], 31, 0x7FFFFFFF, ALU.arith_shift_right,
                                           ALU.bitwise_and))
                    then(dve.tensor_tensor(thr[:, b], key[:, b], sg[:, b], ALU.bitwise_xor))

                threshold()
                a = slice(0, NACT)
                low, high, carry = (half16[:, x, a] for x in range(3))
                counts(lambda i: thr[:, i:i + 1].bitcast(F32), sl, ALU.is_gt, range(NACT))
                done[0] += 1
                dve.wait_ge(sl, done[0])
                then(dve.tensor_scalar(kbit[:, a], cnt[:, a], float(TOPK), None, ALU.is_ge))
                then(dve.tensor_scalar(low, key[:, a], 0xFFFF, None, ALU.bitwise_and))
                then(dve.tensor_tensor(low, low, kbit[:, a], ALU.add))
                then(dve.tensor_scalar(carry, low, 16, None, ALU.logical_shift_right))
                then(dve.tensor_scalar(high, key[:, a], 16, None, ALU.arith_shift_right))
                then(dve.tensor_tensor(high, high, carry, ALU.add))
                then(dve.tensor_scalar(high, high, 16, None, ALU.logical_shift_left))
                then(dve.tensor_scalar(low, low, 0xFFFF, None, ALU.bitwise_and))
                then(dve.tensor_tensor(key[:, a], high, low, ALU.bitwise_or))
                threshold()
                then(dve.tensor_scalar(sg[:, b], thr[:, b], 0x7F800000, None, ALU.bitwise_and))
                then(dve.tensor_scalar(sg[:, b], sg[:, b], 0, -1, ALU.is_gt, ALU.mult))
                then(dve.tensor_tensor(thr[:, b], thr[:, b], sg[:, b], ALU.bitwise_and))
                for i in range(2, NT):
                    w = P * (i + 1)
                    s = g.score[:, soff(i):soff(i + 1)]
                    t = thr[:, i - 2:i - 1].bitcast(F32)
                    o = slice(i - 2, i - 1)
                    dve.tensor_scalar(le[:, 0:w], s, t, None, ALU.is_le, ALU.add, accum_out=cnt[:, o])
                    then(dve.tensor_scalar(eq[:, 0:w], s, t, None, ALU.is_equal))
                    dve.tensor_scalar(need[:, o], cnt[:, o], 1.0, float(TOPK - w), ALU.mult, ALU.add)
                    then(dve.tensor_tensor_scan(cum[:, 0:w], eq[:, 0:w], eq[:, 0:w], 0.0, ALU.add, ALU.max))
                    then(dve.scalar_tensor_tensor(out=eq[:, 0:w], in0=cum[:, 0:w], scalar=need[:, o],
                                                  in1=eq[:, 0:w], op0=ALU.is_le, op1=ALU.mult))
                    then(dve.tensor_tensor(le[:, 0:w], le[:, 0:w], eq[:, 0:w], ALU.subtract))
                    then(dve.scalar_tensor_tensor(out=s, in0=le[:, 0:w], scalar=-BIG, in1=g.dist[:, SEQ - w:SEQ],
                                                  op0=ALU.mult, op1=ALU.min))


def phase2(nc, k, g, scr):
    GRP = [[(G, b) for b in range(4 * G + 3, -1, -1)] for G in range(2)]
    HU = sum(len(x) for x in GRP)
    NU = 2 * HU
    units = [(j, G, b) for j in range(2) for grp in GRP for G, b in grp]
    off = lambda G, b: P * max(0, b - 4 * G)
    first = {}
    n = 0
    for G in range(2):
        for b in range(4 * G + 4):
            first[G, b] = n - off(G, b)
            n += HALF - off(G, b)
    diag = [b >= 4 * G for j, G, b in units]
    R = 4
    ZS = 5
    with ExitStack() as ctx:
        qh = sbuf(nc, ctx, "sb_q_hi2", [P, 2, SEQ], F32R)
        ql = sbuf(nc, ctx, "sb_q_lo2", [P, 2, SEQ], F32R)
        ks = sbuf(nc, ctx, "sb_k_stack", [P, 2, SEQ], F32R)
        vt = sbuf(nc, ctx, "sb_vT_stack", [P, 2, SEQ])
        vs = sbuf(nc, ctx, "sb_v", [P, 2, NT, P], F32R)
        ph = sbuf(nc, ctx, "sp_hi", [P, n], F32R)
        pl = sbuf(nc, ctx, "sp_lo", [P, n], F32R)
        e = sbuf(nc, ctx, "exp_z", [P, R, HALF])
        sp_ = sbuf(nc, ctx, "softplus", [P, R, HALF])
        a = sbuf(nc, ctx, "a_full", [P, R, HALF])
        ah = sbuf(nc, ctx, "a_hi", [P, R, HALF], F32R)
        al = sbuf(nc, ctx, "a_lo", [P, R, HALF], F32R)
        tmp = sbuf(nc, ctx, "o_lo_part", [HD, 2, HALF])
        z = psum(nc, ctx, "ps_z", [P, ZS, HALF])
        o = psum(nc, ctx, "ps_o", [P, 2, HALF])
        tv = psum(nc, ctx, "ps_vt", [P, HALF])

        loaded = k.sems("sb_loaded", 2)
        v_tr = k.sem("sb_v_transposed")
        v_rdy = k.sem("sb_v_ready")
        z_rdy = k.sem("z_ready")
        cl = k.sem("z_clamped")
        ex = k.sem("z_exp")
        ln = k.sem("z_ln")
        mx = k.sem("softplus_ready")
        phr = k.sem("sp_hi_ready")
        plr = k.sem("sp_lo_ready")
        cum = k.sem("sums_added")
        ar = k.sem("a_ready")
        ahr = k.sem("a_hi_ready")
        alr = k.sem("a_lo_ready")
        vd = k.sem("o_added")
        tm = k.sem("o_lo_out")
        od = k.sem("o_stored")

        def at(u):
            return 0 <= u < NU

        def sl(u):
            j, G, b = units[u]
            return slice(off(G, b), HALF)

        def psl(u):
            j, G, b = units[u]
            return slice(first[G, b] + off(G, b), first[G, b] + HALF)

        def group_end(u):
            return units[u][2] == 0

        with nc.Block() as block:
            @block.sync
            def _(sp):
                scr2 = scr.rearrange("t x p n -> (t x p) n")

                def load(i, ahead, j):
                    for dst, t0, parts in ((qh, 0, (0, 0)), (ql, 0, (1, 1)), (ks, 4, (0, 1)), (vt, 8, (0, 1))):
                        for x in range(2):
                            d = dst[HD * x:HD * x + HD, j]
                            r = (2 * t0 + ahead + parts[x]) * P + HD * j
                            src = scr2[r:r + HD, :] if i is None else scr2[bass.ds(i * P + r, HD), :]
                            sp.dma_start(d if dst is vt else d.bitcast(F32), src).then_inc(loaded[j], 16)

                load(None, 0, 0)
                load(None, 0, 1)
                with sp.Fori(0, NH - 2, 2) as i:
                    for j in range(2):
                        sp.wait_ge(vd, i * HU + (HU * (j + 1) + R))
                        load(i, 2, j)

            @block.scalar
            def _(act):
                act.sem_inc(ar, ZS)
                act.preload_act_table_set("natural_log_exp_and_others")
                with act.Fori(0, NH // 2) as it:
                    def step(s):
                        if s in (0, HU):
                            j = s // HU
                            for x in range(2):
                                act.wait_ge(v_tr, it * 4 + (2 * j + x + 1))
                                act.activation(vs[:, j, 4 * x:4 * x + 4, :], tv[:].rearrange("p (b d) -> p b d", b=4),
                                               ACT.Copy).then_inc(v_rdy, 1)
                        u = s
                        if at(u):
                            act.wait_ge(cl, it * NU + (u + 1))
                            act.activation(e[:, u % R, sl(u)], e[:, u % R, sl(u)], ACT.Exp).then_inc(ex, 1)
                        u = s - 3
                        if at(u):
                            act.wait_ge(cum, it * NU + (u + 6))
                            act.wait_ge(alr, it * NU + (u + 1))
                            act.activation(a[:, u % R, sl(u)], z[:, u % ZS, sl(u)], ACT.Exp).then_inc(ar, 1)
                        u = s
                        if at(u):
                            act.wait_ge(ex, it * NU + (u + 1))
                            act.activation(e[:, u % R, sl(u)], e[:, u % R, sl(u)], ACT.Ln, bias=1.0).then_inc(ln, 1)
                        u = s - 7
                        if at(u) and group_end(u):
                            q = sum(group_end(x) for x in range(u))
                            act.wait_ge(vd, it * NU + (u + 1 + R))
                            act.wait_ge(od, it * 4 + (q + 1))
                            act.activation(tmp[:, q % 2], o[HD:P, q % 2], ACT.Copy).then_inc(tm, 1)
                    for s in range(NU + 7):
                        step(s)

            @block.gpsimd
            def _(pool):
                pool.sem_inc(plr, R)
                pool.sem_inc(alr, R)
                with pool.Fori(0, NH // 2) as it:
                    for s in range(NU + 4):
                        u = s - 1
                        if at(u):
                            pool.wait_ge(phr, it * NU + (u + 1))
                            pool.tensor_tensor(pl[:, psl(u)], sp_[:, u % R, sl(u)], ph[:, psl(u)].bitcast(F32),
                                               ALU.subtract).then_inc(plr, 1)
                        u = s - 4
                        if at(u):
                            pool.wait_ge(ahr, it * NU + (u + 1))
                            pool.wait_ge(vd, it * NU + (u + 1))
                            pool.tensor_tensor(al[:, u % R, sl(u)], a[:, u % R, sl(u)], ah[:, u % R, sl(u)].bitcast(F32),
                                               ALU.subtract).then_inc(alr, 1)

            @block.vector
            def _(dve):
                dve.sem_inc(mx, R)
                dve.sem_inc(od, 2)
                with dve.Fori(0, NH // 2) as it:
                    for s in range(-1, NU + 8):
                        u = s - 4
                        if at(u):
                            dve.wait_ge(ar, it * NU + (u + 1 + ZS))
                            dve.wait_ge(vd, it * NU + (u + 1))
                            dve.tensor_copy(ah[:, u % R, sl(u)], a[:, u % R, sl(u)]).then_inc(ahr, 1)
                        u = s - 1
                        if at(u):
                            dve.wait_ge(ln, it * NU + (u + 1))
                            dve.wait_ge(plr, it * NU + (u + 1))
                            dve.tensor_tensor(sp_[:, u % R, sl(u)], z[:, u % ZS, sl(u)], e[:, u % R, sl(u)],
                                              ALU.max).then_inc(mx, 1)
                            dve.wait_ge(mx, it * NU + (u + 1 + R))
                            dve.wait_ge(cum, it * NU + (u + 1))
                            dve.tensor_copy(ph[:, psl(u)], sp_[:, u % R, sl(u)]).then_inc(phr, 1)
                        u = s + 1
                        if at(u):
                            dve.wait_ge(z_rdy, it * NU + (u + 1))
                            dve.wait_ge(mx, it * NU + (u + 1))
                            dve.tensor_scalar(e[:, u % R, sl(u)], z[:, u % ZS, sl(u)], ZCLAMP, None, ALU.min).then_inc(cl, 1)
                        u = s - 7
                        if at(u) and group_end(u):
                            q = sum(group_end(x) for x in range(u))
                            j, G, b = units[u]
                            dve.wait_ge(tm, it * 4 + (q + 1))
                            dve.tensor_tensor(g.osb[HD * j:HD * j + HD, bass.ds(it, 1), HALF * G:HALF * G + HALF]
                                              .rearrange("p a n -> p (a n)"), o[0:HD, q % 2], tmp[:, q % 2],
                                              ALU.add).then_inc(od, 1)

            @block.tensor
            def _(pe):
                pe.sem_inc(v_rdy, 1)
                pe.sem_inc(cum, 5)
                pe.sem_inc(vd, R)
                with pe.Fori(0, NH // 2) as it:
                    for s in range(-1, NU + 6):
                        if s in (-1, HU - 1):
                            j = (s + 1) // HU
                            pe.wait_ge(loaded[j], it * 128 + 128)
                            for x in range(2):
                                pe.wait_ge(v_rdy, it * 4 + (2 * j + x + 1))
                                for b in range(4):
                                    last = pe.transpose(tv[:, P * b:P * b + P],
                                                        vt[:, j, P * (4 * x + b):P * (4 * x + b) + P], g.ident[:])
                                last.then_inc(v_tr, 1)
                        u = s + 1
                        if at(u):
                            j, G, b = units[u]
                            pe.wait_ge(ar, it * NU + (u + 1))
                            q = slice(HALF * G + off(G, b), HALF * G + HALF)
                            kb = ks[:, j, P * b:P * b + P]
                            pe.matmul(z[:, u % ZS, sl(u)], kb, qh[:, j, q], start=True, stop=False)
                            last = pe.matmul(z[:, u % ZS, sl(u)], kb, ql[:, j, q], start=False, stop=True)
                            if diag[u]:
                                d = slice(off(G, b), off(G, b) + P)
                                last = pe.matmul(z[:, u % ZS, d], g.bigid[:], g.tneg[:], start=False, stop=True,
                                                 skip_group_check=True)
                            last.then_inc(z_rdy, 1)
                        u = s - 2
                        if at(u):
                            j, G, b = units[u]
                            pe.wait_ge(plr, it * NU + (u + 1 + R))
                            for c in range(4 * G + 3, b - 1, -1):
                                w = g.tneg if c == b else g.nneg
                                s_ = slice(off(G, c), HALF)
                                for part in (ph, pl):
                                    last = pe.matmul(z[:, u % ZS, s_], w[:], part[:, first[G, c] + off(G, c):first[G, c] + HALF],
                                                     start=False, stop=(c == b and part is pl), skip_group_check=True)
                            last.then_inc(cum, 1)
                        u = s - 6
                        if at(u):
                            j, G, b = units[u]
                            q = sum(group_end(x) for x in range(u))
                            pe.wait_ge(alr, it * NU + (u + 1 + R))
                            if b == 4 * G + 3:
                                pe.wait_ge(od, it * 4 + (q + 1))
                                pe.wait_ge(v_rdy, it * 4 + (2 * j + 3))
                            for part in (ah, al):
                                last = pe.matmul(o[:, q % 2, sl(u)], vs[:, j, b], part[:, u % R, sl(u)],
                                                 start=(b == 4 * G + 3 and part is ah), stop=(b == 0 and part is al),
                                                 skip_group_check=True)
                            last.then_inc(vd, 1)


def phase3(nc, k, g, A, scr, vecs):
    chunks = []
    units = []
    for j in range(2):
        for i in range(NT - 1, -1, -1):
            for c in range(0, i + 1, 4):
                chunks.append((len(units), j, i, c, min(4, i + 1 - c)))
            units.append((j, i))
    NU, NC = len(units), len(chunks)
    last_chunk = [max(q for q in range(NC) if chunks[q][0] == u) for u in range(NU)]
    TS = 4
    with ExitStack() as ctx:
        qs = sbuf(nc, ctx, "d_q_stack", [P, 2, SEQ], F32R)
        nl = sbuf(nc, ctx, "neg_logits", [P, 2, SEQ])
        pe_ = sbuf(nc, ctx, "probs", [P, 2, SEQ])
        th = sbuf(nc, ctx, "pT_hi", [P, TS, HALF], F32R)
        tl = sbuf(nc, ctx, "pT_lo", [P, TS, HALF], F32R)
        nm = sbuf(nc, ctx, "neg_max", [P, 2])
        sm = sbuf(nc, ctx, "prob_sum", [P, 4])
        rs = sbuf(nc, ctx, "prob_rsum", [P, 4])
        ns = sbuf(nc, ctx, "head_nslope", [P, 2])
        tmp = sbuf(nc, ctx, "od_lo_part", [P, 2, HD])
        acc = sbuf(nc, ctx, "mod_acc_b", [P, 12, 512])
        prod = sbuf(nc, ctx, "mod_prod", [P, 2, 512])
        mb = sbuf(nc, ctx, "mb2", [P, 16])
        with ExitStack() as c:
            wm = sbuf(nc, c, "wmod_b", [P, 4, KD, 512])
        with ExitStack() as c:
            row = sbuf(nc, c, "mod_rows", [1, 5, D])
        z = psum(nc, ctx, "ps_dz", [P, 2, SEQ])
        tr = psum(nc, ctx, "ps_dt", [P, 2, HALF])
        o = psum(nc, ctx, "ps_do", [P, 2, HALF])

        loaded = k.sems("d_loaded", 2)
        zr = k.sem("dz_ready")
        nsr = k.sem("d_slope_ready")
        seen = k.sem("dz_seen")
        tt = k.sem("neg_logits_ready")
        ex = k.sem("probs_ready")
        td = k.sem("p_transposed")
        thr = k.sem("pT_hi_ready")
        tlr = k.sem("pT_lo_ready")
        vd = k.sem("d_o_added")
        rc = k.sem("d_rsum_ready")
        f1 = k.sem("d_lo_out")
        oo = k.sem("d_o_stored")

        wm_loaded = k.sems("wmb_loaded", 4)
        row_loaded = k.sem("row_bias_loaded")
        chain = k.sem("modb_first_product")
        pr = k.sem("modb_product")
        summed = k.sem("modb_summed")
        accd = k.sem("modb_acc_done")
        accv = k.sem("modb_acc_done_dve")
        accp = k.sem("modb_acc_step_dve")
        colm = k.sem("mod2_summed")
        rowm = k.sem("row_summed")
        mbs = k.sem("mod2_biased")
        rowd = k.sem("row_ready")
        row_stored = k.sem("row_stored")
        mods = [(A["w_mod"][0], 2 * D + 512 * c) for c in range(8)] + [(A["w_mod_final"], 512 * c) for c in range(4)]
        rows = [(0, 0, 0, tr[0:1, 0]), (1, 0, 1, tr[0:1, 1]), (6, 1, 0, z[0:1, 0, HALF:]), (7, 1, 1, z[0:1, 1, 0:HALF]),
                (8, 2, 0, z[0:1, 1, HALF:]), (9, 2, 1, o[0:1, 0]), (10, 3, 0, o[0:1, 1]), (11, 3, 1, z[0:1, 0, 0:HALF])]
        STEPS = NH // 2
        NPOOL = len(mods) - NH

        def of(u):
            return [q for q in range(NC) if chunks[q][0] == u]

        with nc.Block() as block:
            @block.sync
            def _(sp):
                scr2 = scr.rearrange("t x p n -> (t x p) n")

                def load(i, row, j):
                    for x in range(2):
                        r = (12 * 2 + x) * P + HD * j + row
                        src = scr2[r:r + HD, :] if i is None else scr2[bass.ds(i * 2 * P + r, HD), :]
                        sp.dma_start(qs[HD * x:HD * x + HD, j].bitcast(F32), src).then_inc(loaded[j], 16)

                for j in range(2):
                    load(None, 0, j)

                def load_mod(c):
                    if c >= 2:
                        sp.wait_ge(accd, c - 1)
                    w, col = mods[c]
                    sp.dma_start(wm[:, c % 2], w.rearrange("(t p) n -> p t n", p=P)[:, :, col:col + 512])\
                      .then_inc(wm_loaded[c % 2], 16)

                def load_mod_dve(n):
                    if n >= 2:
                        sp.wait_ge(accv, n - 1)
                    w, col = mods[NPOOL + n]
                    sp.dma_start(wm[:, 2 + n % 2], w.rearrange("(t p) n -> p t n", p=P)[:, :, col:col + 512])\
                      .then_inc(wm_loaded[2 + n % 2], 16)

                load_mod(0)
                load_mod_dve(0)
                load_mod(1)
                load_mod_dve(1)
                for h in range(2, NH):
                    sp.wait_ge(zr, NT * (h - 1))
                    load(None, (h // 2) * 2 * P, h % 2)
                    load_mod_dve(h)
                    if h < NPOOL:
                        load_mod(h)
                sp.wait_ge(accd, NPOOL)
                for r, b in enumerate((A["b_mod"][0:1, 2 * D:3 * D], A["b_mod"][0:1, 5 * D:6 * D],
                                       A["b_mod_final"][0:D].unsqueeze(0), A["b_mod_final"][D:2 * D].unsqueeze(0),
                                       A["final_gain"].unsqueeze(0))):
                    sp.dma_start(row[:, r], b).then_inc(row_loaded, 16)
                sp.wait_ge(rowd, 10)
                sp.dma_start(vecs.rearrange("(o r) n -> o r n", o=1), row[:, 0:4]).then_inc(row_stored, 16)
                sp.wait_ge(row_stored, 16)

            @block.gpsimd
            def _(pool):
                for c in range(NPOOL):
                    pool.wait_ge(wm_loaded[c % 2], 16 * (c // 2 + 1))
                    pool.tensor_scalar(acc[:, c], wm[:, c % 2, 0], g.csil[:, 0:1], None, ALU.mult).then_inc(chain, 1)
                    for t in range(1, KD):
                        n = 7 * c + t - 1
                        if n >= 2:
                            pool.wait_ge(summed, n - 1)
                        pool.tensor_scalar(prod[:, n % 2], wm[:, c % 2, t], g.csil[:, t:t + 1], None, ALU.mult)\
                            .then_inc(pr, 1)
                        pool.wait_ge(pr, n + 1)
                        if t == 1:
                            pool.wait_ge(chain, c + 1)
                        else:
                            pool.wait_ge(summed, n)
                        ins = pool.tensor_tensor(acc[:, c], acc[:, c], prod[:, n % 2], ALU.add)
                        ins.then_inc(summed, 1)
                    pool.wait_ge(summed, 7 * c + 7)
                    pool.sem_inc(accd, 1)

            @block.scalar
            def _(act):
                act.sem_inc(ex, 2)
                with act.Fori(0, NH // 2) as it:
                    for s in range(NU + 3):
                        if s < NU:
                            j, i = units[s]
                            w = P * (i + 1)
                            act.wait_ge(tt, it * NU + (s + 3))
                            act.wait_ge(td, it * NC + (last_chunk[s - 2] + 2 if s >= 2 else 1))
                            act.activation(pe_[:, s % 2, 0:w], nl[:, s % 2, 0:w], ACT.Exp, scale=-1.0,
                                           bias=nm[:, s % 2:s % 2 + 1], accum_out=sm[:, s % 4:s % 4 + 1]).then_inc(ex, 1)
                        for q in of(s - 1):
                            w = P * chunks[q][4]
                            act.wait_ge(td, it * NC + (q + 2))
                            act.wait_ge(vd, it * NC + (q + 1))
                            act.activation(th[:, q % TS, 0:w], tr[:, q % 2, 0:w], ACT.Copy).then_inc(thr, 1)
                        u = s - 3
                        if u >= 0:
                            act.wait_ge(rc, it * NU + (u + 1))
                            act.wait_ge(oo, it * NU + (u + 1))
                            act.wait_ge(vd, it * NC + (last_chunk[u] + 1 + TS))
                            act.activation(tmp[:, u % 2], o[:, u % 2, HD:P], ACT.Copy,
                                           scale=rs[:, u % 4:u % 4 + 1]).then_inc(f1, 1)

            @block.vector
            def _(dve):
                dve.sem_inc(tt, 2)
                dve.sem_inc(tlr, 2)
                dve.sem_inc(oo, 2)
                with dve.Fori(0, NH // 2) as it:
                    for j in range(2):
                        dve.wait_ge(tt, it * NU + 2)
                        dve.tensor_copy(ns[:, j:j + 1], g.nslope[:, bass.ds(it * 2 + j, 1)]).then_inc(nsr, 1)
                    dve.wait_ge(nsr, it * 2 + 2)

                    for s in range(-1, NU + 3):
                        u = s + 1
                        if u < NU:
                            j, i = units[u]
                            w = P * (i + 1)
                            dve.wait_ge(zr, it * NU + (u + 1))
                            dve.wait_ge(ex, it * NU + (u + 1))
                            dve.sem_inc(seen, 1)
                            dve.tensor_tensor_reduce(nl[:, u % 2, 0:w], z[:, u % 2, 0:w], g.score[:, soff(i):soff(i + 1)],
                                                     ns[:, j:j + 1], 3e38, ALU.add, ALU.min,
                                                     nm[:, u % 2:u % 2 + 1]).then_inc(tt, 1)
                        for q in of(s - 1):
                            w = P * chunks[q][4]
                            dve.wait_ge(thr, it * NC + (q + 1))
                            dve.tensor_tensor(tl[:, q % TS, 0:w], tr[:, q % 2, 0:w], th[:, q % TS, 0:w].bitcast(F32),
                                              ALU.subtract).then_inc(tlr, 1)
                        u = s - 1
                        if 0 <= u < NU:
                            dve.wait_ge(ex, it * NU + (u + 3))
                            dve.wait_ge(oo, it * NU + max(1, u - 1))
                            dve.reciprocal(rs[:, u % 4:u % 4 + 1], sm[:, u % 4:u % 4 + 1]).then_inc(rc, 1)
                        u = s - 3
                        if u >= 0:
                            j, i = units[u]
                            dve.wait_ge(f1, it * NU + (u + 1))
                            dve.scalar_tensor_tensor(out=g.otok[:, i, bass.ds(it * P + HD * j, HD)], in0=o[:, u % 2, 0:HD],
                                                     scalar=rs[:, u % 4:u % 4 + 1], in1=tmp[:, u % 2], op0=ALU.mult,
                                                     op1=ALU.add).then_inc(oo, 1)
                        if 0 <= s < NU:
                            c, t = s // KD, s % KD
                            x = acc[:, bass.ds(it * 2 + NPOOL + c, 1), :].rearrange("p a n -> p (a n)")
                            if t == 0:
                                dve.wait_ge(wm_loaded[2 + c], it * 16 + 16)
                                ins = dve.tensor_scalar(x, wm[:, 2 + c, t], g.csil[:, 0:1], None, ALU.mult)
                            else:
                                dve.wait_ge(accp, it * (2 * KD - 2) + (KD - 1) * c + t)
                                ins = dve.scalar_tensor_tensor(out=x, in0=wm[:, 2 + c, t], scalar=g.csil[:, t:t + 1],
                                                               in1=x, op0=ALU.mult, op1=ALU.add)
                            ins.then_inc(accp if t < KD - 1 else accv, 1)
                dve.wait_ge(colm, 1)
                dve.tensor_tensor(mb[:], z[:, 0, 0:16], g.cols[:, 24:40], ALU.add).then_inc(mbs, 1)
                dve.wait_ge(mbs, 1)
                dve.tensor_copy(g.b2[:], mb[:, 0:8]).then_inc(mbs, 1)
                dve.scalar_tensor_tensor(out=g.a2[:], in0=mb[:, 8:16], scalar=1.0, in1=g.cols[:, R_N2:R_N2 + 8],
                                         op0=ALU.add, op1=ALU.mult).then_inc(mbs, 1)
                dve.wait_ge(row_loaded, 16 * 5)
                for n, (c, r, half, ps) in enumerate(rows):
                    x = slice(HALF * half, HALF * half + HALF)
                    dve.wait_ge(rowm, n + 1)
                    dve.tensor_tensor(row[:, r, x], ps, row[:, r, x], ALU.add).then_inc(rowd, 1)
                dve.wait_ge(rowd, len(rows))
                for half in range(2):
                    x = slice(HALF * half, HALF * half + HALF)
                    dve.scalar_tensor_tensor(out=row[:, 3, x], in0=row[:, 3, x], scalar=1.0, in1=row[:, 4, x],
                                             op0=ALU.add, op1=ALU.mult).then_inc(rowd, 1)

            @block.tensor
            def _(pe):
                pe.sem_inc(vd, TS)
                pe.sem_inc(td, 1)
                with pe.Fori(0, NH // 2) as it:
                    for s in range(-1, NU + 2):
                        u = s + 1
                        if u < NU:
                            j, i = units[u]
                            w = P * (i + 1)
                            if i == NT - 1:
                                pe.wait_ge(loaded[j], it * 32 + 32)
                            pe.wait_ge(tt, it * NU + (u + 1))
                            qb = qs[:, j, P * i:P * i + P]
                            for c in range(0, w, HALF):
                                x = slice(c, min(c + HALF, w))
                                pe.matmul(z[:, u % 2, x], qb, g.kdh[:, x], start=True, stop=False)
                                last = pe.matmul(z[:, u % 2, x], qb, g.kdl[:, x], start=False, stop=True)
                            last.then_inc(zr, 1)
                        for q in of(s - 1):
                            u, j, i, c, m = chunks[q]
                            pe.wait_ge(ex, it * NU + (u + 3))
                            pe.wait_ge(tlr, it * NC + (q + 1))
                            for b in range(m):
                                last = pe.transpose(tr[:, q % 2, P * b:P * b + P],
                                                    pe_[:, u % 2, P * (c + b):P * (c + b) + P], g.ident[:])
                            last.then_inc(td, 1)
                        for q in of(s - 2):
                            u, j, i, c, m = chunks[q]
                            pe.wait_ge(tlr, it * NC + (q + 3))
                            if c == 0:
                                pe.wait_ge(oo, it * NU + (u + 1))
                            for b in range(m):
                                for part in (th, tl):
                                    last = pe.matmul(o[:, u % 2, 0:P], part[:, q % TS, P * b:P * b + P], g.vd[:, c + b],
                                                     start=(c + b == 0 and part is th), stop=(c + b == i and part is tl))
                            last.then_inc(vd, 1)
                pe.wait_ge(tt, STEPS * NU + 2)
                pe.wait_ge(tlr, STEPS * NC + 2)
                pe.wait_ge(oo, STEPS * NU + 2)
                pe.wait_ge(accd, NPOOL)
                pe.wait_ge(accv, 2)
                for n in range(16):
                    m = pe.matmul(z[:, 0, n:n + 1], acc[:, 2 + n // 4, P * (n % 4):P * (n % 4) + P], g.ones[:, 0:1],
                                  start=(n == 0), stop=True, skip_group_check=True)
                m.then_inc(colm, 1)
                pe.wait_ge(accv, NH)
                for c, r, half, ps in rows:
                    if c == len(mods) - 1:
                        pe.wait_ge(mbs, 1)
                    pe.matmul(ps, g.ones[:, 0:1], acc[:, c], start=True, stop=True).then_inc(rowm, 1)


def phase4(nc, k, g, A, vecs):
    NF = 2 * KD
    with ExitStack() as ctx:
        wl = sbuf(nc, ctx, "wo_lo", [P, KD, D], F32R)
        wh = sbuf(nc, ctx, "wo_hi", [P, KD, D], F32R)
        oh = sbuf(nc, ctx, "oT_hi", [P, KD, SEQ], F32R)
        ol = sbuf(nc, ctx, "oT_lo", [P, KD, SEQ], F32R)
        g1 = sbuf(nc, ctx, "gate1", [P, D])
        sq = sbuf(nc, ctx, "o_sq", [P, 2, HALF])
        hf = sbuf(nc, ctx, "o_full", [P, 2, HALF])
        rb = sbuf(nc, ctx, "sb_rstd", [P, HALF])
        s4 = sbuf(nc, ctx, "sb_ss", [P, 4 * NT])
        rc = sbuf(nc, ctx, "sb_rstd_col", [P, NT])
        ss = sbuf(nc, ctx, "d_ss", [P, NT])
        ps_s = psum(nc, ctx, "ps_ss", [P, 2, HALF])
        ps_t = psum(nc, ctx, "ps_ot", [P, 2, HALF])
        ps_y = psum(nc, ctx, "ps_y", [P, 4, HALF])

        x_loaded = k.sems("x1_loaded", NT)
        wo_loaded = k.sems("wo_loaded", KD)
        g1_loaded = k.sem("gate1_loaded")
        whr = k.sem("wo_hi_ready")
        wlr = k.sem("wo_lo_ready")
        dss = k.sem("d_ss_ready")
        dsn = k.sem("d_ss_scaled")
        drs = k.sem("d_rstd_ready")
        dsc = k.sem("d_scaled")
        sqd = k.sem("o_sq_ready")
        sqm = k.sem("o_sq_summed")
        ssr = k.sem("sb_ss_ready")
        svr = k.sem("sb_var_ready")
        dgr = k.sem("diag_ready")
        spr = k.sem("rstd_spread")
        rbr = k.sem("sb_rstd_spread_ready")
        srs = k.sem("sb_rstd_ready")
        tr = k.sem("o_transposed")
        hfr = k.sem("o_full_ready")
        hfd = k.sem("o_full_ready_dsa")
        ohr = k.sem("oT_hi_ready")
        olr = k.sem("oT_lo_ready")
        ym = k.sem("y_summed")
        yg = k.sem("y_gated")
        x1r = k.sem("x1_ready")
        s2 = k.sem("ss2_ready")
        xb = A["x"][0].rearrange("(i p) d -> i p d", p=P)
        half = lambda h: slice(HALF * h, HALF * h + HALF)

        with nc.Block() as block:
            @block.sync
            def _(sp):
                for t in range(KD):
                    sp.dma_start(g.x1[:, t], A["w_o"][0][P * t:P * t + P, :]).then_inc(wo_loaded[t], 16)
                sp.dma_start(g1[:], vecs[0:1, :].partition_broadcast(P)).then_inc(g1_loaded, 16)
                for i in range(NT):
                    sp.wait_ge(wlr, i + 1)
                    sp.dma_start(g.x1[:, i], xb[i]).then_inc(x_loaded[i], 16)

            @block.scalar
            def _(act):
                for i in range(NT):
                    if i >= 2:
                        act.wait_ge(dss, i - 1)
                    act.activation(hf[:, i % 2], g.otok[:, i], ACT.Square, accum_out=ss[:, i:i + 1]).then_inc(dss, 1)
                def w_hi(t):
                    act.wait_ge(wo_loaded[t], 16)
                    act.activation(wh[:, t], g.x1[:, t], ACT.Copy).then_inc(whr, 1)

                for i in range(NT):
                    act.wait_ge(drs, 1)
                    act.activation(g.otok[:, i], g.otok[:, i], ACT.Copy, scale=ss[:, i:i + 1]).then_inc(dsc, 1)
                    if i % 2:
                        w_hi(i // 2)
                for h in range(2):
                    for f in range(4):
                        n = KD * h + 4 + f
                        act.wait_ge(tr, 4 * h + f + 1)
                        act.wait_ge(dss, NT)
                        act.wait_ge(olr, n - 1)
                        act.activation(hf[:, n % 2], ps_t[:, f % 2], ACT.Copy,
                                       scale=g.cols[:, R_DG + f:R_DG + f + 1]).then_inc(hfd, 1)
                    if h == 0:
                        for t in range(4, KD):
                            w_hi(t)
                for i in range(NT):
                    act.wait_ge(x1r, 2 * i + 2)
                    if i >= 1:
                        act.wait_ge(s2, i)
                    act.activation(g.otok[:, 0:2], g.x1[:, i].rearrange("p (a n) -> p a n", a=2), ACT.Square,
                                   accum_out=g.ss2[:, i:i + 1]).then_inc(s2, 1)

            @block.gpsimd
            def _(pool):
                pool.wait_ge(dss, NT)
                pool.tensor_scalar(ss[:], ss[:], 1.0 / (NH * HD), EPS, ALU.mult, ALU.add).then_inc(dsn, 1)
                pool.wait_ge(dsn, 1)
                pool.tensor_tensor(ss[:], ss[:], g.nhalf[:], ALU.pow).then_inc(drs, 1)
                pool.wait_ge(svr, 1)
                pool.tensor_tensor(rc[:], rc[:], g.nhalf[:], ALU.pow).then_inc(srs, 1)
                for t in range(KD):
                    pool.wait_ge(whr, t + 1)
                    pool.tensor_tensor(wl[:, t], g.x1[:, t], wh[:, t].bitcast(F32), ALU.subtract)\
                        .then_inc(wlr, 1)

            @block.tensor
            def _(pe):
                def sum_sb(n):
                    h, f = n // NPAIR, n % NPAIR
                    pe.wait_ge(sqd, n + 1)
                    for b in range(4):
                        m = pe.matmul(ps_s[:, 0, NT * f + 4 * h + b:NT * f + 4 * h + b + 1],
                                      sq[:, n % 2, P * b:P * b + P], g.ones[:, 0:1], start=(n == 0 and b == 0),
                                      stop=True, skip_group_check=True)
                    m.then_inc(sqm, 1)

                def spread(h):
                    for b in range(4):
                        pe.wait_ge(dgr, 4 * h + b + 1)
                        m = pe.matmul(ps_s[:, 1, P * b:P * b + P], g.ones[:], sq[:, b % 2, 0:P], start=(b == 0), stop=True,
                                      skip_group_check=True)
                        m.then_inc(spr, 1)

                def transposes(h):
                    pe.wait_ge(dsc, 4 * h + 4)
                    for f in range(4):
                        n = 4 * h + f
                        if n >= 2:
                            pe.wait_ge(hfd, n - 1)
                        for b in range(4):
                            m = pe.transpose(ps_t[:, f % 2, P * b:P * b + P], g.otok[:, 4 * h + b, P * f:P * f + P],
                                             g.ident[:])
                        m.then_inc(tr, 1)

                for n in range(2 * NPAIR):
                    sum_sb(n)
                spread(0)
                transposes(0)
                pe.wait_ge(rbr, 1)
                spread(1)
                for i in range(NT):
                    if i == 1:
                        transposes(1)
                    pe.wait_ge(olr, KD * (i // 4) + KD)
                    b = slice(P * i, P * i + P)
                    for c in range(2):
                        n = 2 * i + c
                        if n >= 4:
                            pe.wait_ge(yg, n - 3)
                        for t in range(KD):
                            if n == 0:
                                pe.wait_ge(wlr, t + 1)
                            for x, w in ((oh, wh), (oh, wl), (ol, wh)):
                                m = pe.matmul(ps_y[:, n % 4], x[:, t, b], w[:, t, half(c)],
                                              start=(t == 0 and x is oh and w is wh), stop=(t == KD - 1 and x is ol))
                        m.then_inc(ym, 1)

            @block.vector
            def _(dve):
                def split(n):
                    h, f = n // KD, n % KD
                    dve.wait_ge(hfr, n + 1)
                    dve.tensor_copy(oh[:, f, half(h)], hf[:, n % 2]).then_inc(ohr, 1)
                    dve.wait_ge(ohr, n + 1)
                    dve.tensor_tensor(ol[:, f, half(h)], hf[:, n % 2], oh[:, f, half(h)].bitcast(F32),
                                      ALU.subtract).then_inc(olr, 1)

                for n in range(2 * NPAIR):
                    h, f = n // NPAIR, n % NPAIR
                    if n >= 2:
                        dve.wait_ge(sqm, n - 1)
                    dve.tensor_tensor(sq[:, n % 2], g.osb[:, f, half(h)], g.osb[:, f, half(h)], ALU.mult)\
                       .then_inc(sqd, 1)
                dve.wait_ge(sqm, 2 * NPAIR)
                dve.tensor_copy(s4[:], ps_s[:, 0, 0:4 * NT]).then_inc(ssr, 1)
                for n in range(3):
                    dve.wait_ge(ssr, n + 1)
                    dve.tensor_tensor(s4[:, 0:NT], s4[:, 0:NT], s4[:, NT * (n + 1):NT * (n + 2)], ALU.add).then_inc(ssr, 1)
                dve.wait_ge(ssr, 4)
                dve.tensor_scalar(rc[:], s4[:, 0:NT], 1.0 / (NH * HD), EPS, ALU.mult, ALU.add).then_inc(svr, 1)
                for h in range(2):
                    dve.wait_ge(srs, 1)
                    for b in range(4):
                        n = 4 * h + b
                        if n >= 2:
                            dve.wait_ge(spr, n - 1)
                        dve.tensor_scalar(sq[:, b % 2, 0:P], g.ident[:], rc[:, n:n + 1], None, ALU.mult).then_inc(dgr, 1)
                    dve.wait_ge(spr, 4 * h + 4)
                    if h == 1:
                        dve.wait_ge(olr, KD)
                    dve.tensor_copy(rb[:], ps_s[:, 1]).then_inc(rbr, 1)
                    dve.wait_ge(rbr, h + 1)
                    dve.wait_ge(dss, NT)
                    for f in range(NPAIR):
                        n = KD * h + f
                        if n >= 2:
                            dve.wait_ge(olr, n - 1)
                        dve.scalar_tensor_tensor(out=hf[:, n % 2], in0=g.osb[:, f, half(h)],
                                                 scalar=g.cols[:, R_SBG + f:R_SBG + f + 1], in1=rb[:],
                                                 op0=ALU.mult, op1=ALU.mult).then_inc(hfr, 1)
                        split(n)
                    for f in range(4):
                        dve.wait_ge(hfd, 4 * h + f + 1)
                        dve.sem_inc(hfr, 1)
                        split(KD * h + 4 + f)
                dve.wait_ge(g1_loaded, 16)
                for i in range(NT):
                    dve.wait_ge(x_loaded[i], 16)
                    for c in range(2):
                        n = 2 * i + c
                        dve.wait_ge(ym, n + 1)
                        if n == 0:
                            dve.wait_ge(olr, 2 * KD)
                        else:
                            dve.wait_ge(x1r, n)
                        dve.tensor_tensor(hf[:, n % 2], ps_y[:, n % 4], g1[:, half(c)], ALU.mult).then_inc(yg, 1)
                        dve.wait_ge(yg, n + 1)
                        dve.tensor_tensor(g.x1[:, i, half(c)], g.x1[:, i, half(c)], hf[:, n % 2], ALU.add)\
                           .then_inc(x1r, 1)


def phase5(nc, k, g, A, vecs, out):
    MC = 2
    NCH = NM // MC
    UN = 2 * MC
    half = lambda h: slice(HALF * h, HALF * h + HALF)
    with ExitStack() as ctx:
        hh = sbuf(nc, ctx, "h2T_hi", [P, KD, SEQ], F32R)
        hl = sbuf(nc, ctx, "h2T_lo", [P, KD, SEQ], F32R)
        g2 = sbuf(nc, ctx, "gate2", [P, D])
        wr = sbuf(nc, ctx, "wgu_raw", [P, MC, 2, KD, P])
        wh = sbuf(nc, ctx, "wgu_hi", [P, MC, 2, KD, P], F32R)
        wl = sbuf(nc, ctx, "wgu_lo", [P, MC, 2, KD, P], F32R)
        dr = sbuf(nc, ctx, "wd_raw", [P, MC, D])
        dh = sbuf(nc, ctx, "wd_hi", [P, MC, D], F32R)
        dl = sbuf(nc, ctx, "wd_lo", [P, MC, D], F32R)
        sg = sbuf(nc, ctx, "silu_gate", [P, 2, HALF])
        af = sbuf(nc, ctx, "act_full", [P, 2, HALF])
        ssv = sbuf(nc, ctx, "ssv2", [P, NT])
        rstd = sbuf(nc, ctx, "rstd2", [P, NT])
        ssf = sbuf(nc, ctx, "ssf", [P, NT])
        rf = sbuf(nc, ctx, "rstdf", [P, NT])
        with ExitStack() as c:
            xh = sbuf(nc, c, "xhat", [P, 4, D])
        with ExitStack() as c:
            ah = sbuf(nc, c, "act_hi", [P, MC, SEQ], F32R)
            al = sbuf(nc, c, "act_lo", [P, MC, SEQ], F32R)
        afin, bfin = (wr[:, 0, j].rearrange("p t n -> p (t n)") for j in range(2))
        ps_g = psum(nc, ctx, "ps_gate", [P, 2, HALF])
        ps_u = psum(nc, ctx, "ps_up", [P, 2, HALF])
        ps_d = psum(nc, ctx, "ps_down", [P, 4, HALF])

        g2_loaded = k.sem("gate2_loaded")
        wr_loaded = k.sems("wgu_loaded", MC)
        dr_loaded = k.sem("wd_loaded")
        ssn = k.sem("ss2_scaled")
        rs = k.sem("rstd2_ready")
        xhr = k.sem("xhat2_ready")
        tr = k.sem("x1_transposed")
        hfr = k.sem("h2_full_ready")
        hir = k.sem("h2_hi_ready")
        lor = k.sem("h2_lo_ready")
        gu = k.sem("gate_up_summed")
        whr = k.sem("wgu_hi_ready")
        wlr = k.sem("wgu_lo_ready")
        sil = k.sem("silu_ready")
        gat = k.sem("act_full_ready")
        ahr = k.sem("act_hi_ready")
        alr = k.sem("act_lo_ready")
        dsc = k.sem("wd_scaled")
        dhr = k.sem("wd_hi_ready")
        dlr = k.sem("wd_lo_ready")
        dm = k.sem("down_summed")
        add = k.sem("down_added")
        sf = k.sem("ssf_ready")
        sfn = k.sem("ssf_scaled")
        rfr = k.sem("rstdf_ready")
        ab_loaded = k.sem("final_vectors_loaded")
        om = k.sem("out_scaled")
        od = k.sem("out_ready_dve")
        op = k.sem("out_ready_pool")
        stored = k.sem("out_stored")
        ob = out[0].rearrange("(i p) d -> i p d", p=P)
        ND = 2 * NT

        with nc.Block() as block:
            @block.sync
            def _(sp):
                w = [A[n][0].rearrange("(t p) n -> p t n", p=P) for n in ("w_gate", "w_up")]
                wd = A["w_down"][0]

                def load_gu(it, m):
                    for j in range(2):
                        x = w[j][:, :, P * m:P * m + P] if it is None else w[j][:, :, bass.ds(it * (MC * P) + P * m, P)]
                        sp.dma_start(wr[:, m, j], x).then_inc(wr_loaded[m], 16)

                def load_d(it):
                    x = wd[0:MC * P, :] if it is None else wd[bass.ds(it * (MC * P), MC * P), :]
                    sp.dma_start(dr[:], x.rearrange("(m p) n -> p m n", p=P)).then_inc(dr_loaded, 16)

                for m in range(MC):
                    load_gu(None, m)
                sp.dma_start(g2[:], vecs[1:2, :].partition_broadcast(P)).then_inc(g2_loaded, 16)
                load_d(None)
                with sp.Fori(1, NCH) as it:
                    for m in range(MC):
                        sp.wait_ge(wlr, it * MC + (m + 1))
                        load_gu(it, m)
                    sp.wait_ge(dlr, it + 1)
                    load_d(it)
                sp.wait_ge(wlr, NCH * MC + 1)
                sp.dma_start(bfin, vecs[2:3, :].partition_broadcast(P)).then_inc(ab_loaded, 16)
                sp.dma_start(afin, vecs[3:4, :].partition_broadcast(P)).then_inc(ab_loaded, 16)
                for i in range(NT):
                    sp.wait_ge(op if i % 2 else od, i // 2 + 1)
                    sp.dma_start(ob[i], g.x1[:, i]).then_inc(stored, 16)
                sp.wait_ge(stored, 16 * NT)

            @block.scalar
            def _(act):
                def w_hi(it, m):
                    act.wait_ge(wr_loaded[m], it * 32 + 32)
                    act.wait_ge(gu, it * UN + (2 * m + 2))
                    act.activation(wh[:, m], wr[:, m], ACT.Copy).then_inc(whr, 1)

                def gate(it, u):
                    act.wait_ge(gu, it * UN + (u + 1 + 4))
                    act.wait_ge(gat, it * UN + (u + 1))
                    act.activation(sg[:, u % 2], ps_g[:, u % 2], ACT.Silu).then_inc(sil, 1)

                def d_hi(it):
                    act.wait_ge(dsc, it + 1)
                    act.wait_ge(dm, it * ND + ND)
                    act.activation(dh[:], dr[:], ACT.Copy).then_inc(dhr, 1)

                act.wait_ge(rs, 1)
                for h in range(2):
                    for b in range(4):
                        i = 4 * h + b
                        if h == 1:
                            act.wait_ge(tr, KD)
                        act.activation(xh[:, b], g.x1[:, i], ACT.Copy, scale=rstd[:, i:i + 1]).then_inc(xhr, 1)
                    for t in range(KD):
                        n = KD * h + t
                        act.wait_ge(tr, n + 1)
                        if n >= 2:
                            act.wait_ge(lor, n - 1)
                        act.activation(sg[:, n % 2], ps_d[:, n % 4], ACT.Identity, bias=g.b2[:, t:t + 1],
                                       scale=g.a2[:, t:t + 1]).then_inc(hfr, 1)
                        if n in (2, 4):
                            w_hi(0, n // 2 - 1)
                act.wait_ge(lor, 2 * KD)
                with act.Fori(0, NCH - 1) as it:
                    gate(it, 0)
                    d_hi(it)
                    gate(it, 1)
                    w_hi(it + 1, 0)
                    gate(it, 2)
                    gate(it, 3)
                    w_hi(it + 1, 1)
                gate(NCH - 1, 0)
                d_hi(NCH - 1)
                for u in range(1, UN):
                    gate(NCH - 1, u)
                for i in range(NT):
                    act.wait_ge(add, (NCH - 1) * ND + 2 * i + 2 + 4)
                    if i >= 1:
                        act.wait_ge(sf, i)
                    act.activation(sg[:], g.x1[:, i].rearrange("p (a n) -> p a n", a=2), ACT.Square,
                                   accum_out=ssf[:, i:i + 1]).then_inc(sf, 1)

            @block.gpsimd
            def _(pool):
                pool.sem_inc(wlr, MC)
                pool.sem_inc(dlr, 1)
                pool.tensor_scalar(ssv[:], g.ss2[:], 1.0 / D, EPS, ALU.mult, ALU.add).then_inc(ssn, 1)
                pool.wait_ge(ssn, 1)
                pool.tensor_tensor(rstd[:], ssv[:], g.nhalf[:], ALU.pow).then_inc(rs, 1)

                def w_lo(it, m):
                    pool.wait_ge(whr, it * MC + (m + 1))
                    pool.tensor_tensor(wl[:, m], wr[:, m], wh[:, m].bitcast(F32), ALU.subtract).then_inc(wlr, 1)

                def d_lo(it):
                    pool.wait_ge(dhr, it + 1)
                    pool.tensor_tensor(dl[:], dr[:], dh[:].bitcast(F32), ALU.subtract).then_inc(dlr, 1)

                for m in range(MC):
                    w_lo(0, m)
                with pool.Fori(0, NCH - 1) as it:
                    d_lo(it)
                    for m in range(MC):
                        w_lo(it + 1, m)
                d_lo(NCH - 1)
                pool.wait_ge(ab_loaded, 32)
                for i in range(NT):
                    pool.wait_ge(sf, i + 1)
                    s = slice(i, i + 1)
                    pool.tensor_scalar(ssf[:, s], ssf[:, s], 1.0 / D, EPS, ALU.mult, ALU.add).then_inc(sfn, 1)
                    pool.wait_ge(sfn, i + 1)
                    pool.tensor_tensor(rf[:, s], ssf[:, s], g.nhalf[:, 0:1], ALU.pow).then_inc(rfr, 1)
                    if i % 2:
                        pool.wait_ge(om, i + 1)
                        pool.tensor_tensor(g.x1[:, i], g.x1[:, i], bfin, ALU.add).then_inc(op, 1)

            @block.tensor
            def _(pe):
                pe.sem_inc(gu, 4)
                pe.sem_inc(dm, ND)
                for n in range(2 * KD):
                    h, t = n // KD, n % KD
                    pe.wait_ge(xhr, 4 * h + 4)
                    if n >= 4:
                        pe.wait_ge(hfr, n - 3)
                    for b in range(4):
                        m = pe.transpose(ps_d[:, n % 4, P * b:P * b + P], xh[:, b, P * t:P * t + P], g.ident[:])
                    m.then_inc(tr, 1)
                pe.wait_ge(lor, KD)
                with pe.Fori(0, NCH) as it:
                    for m in range(MC):
                        pe.wait_ge(wlr, it * MC + (m + 1 + MC))
                        for h in range(2):
                            u = 2 * m + h
                            if u == 1:
                                pe.wait_ge(lor, 2 * KD)
                            pe.wait_ge(gat, it * UN + (u + 1))
                            for j, ps in ((0, ps_g), (1, ps_u)):
                                for t in range(KD):
                                    for w, x in ((wh, hh), (wh, hl), (wl, hh)):
                                        last = pe.matmul(ps[:, u % 2], w[:, m, j, t], x[:, t, half(h)],
                                                         start=(t == 0 and w is wh and x is hh),
                                                         stop=(t == KD - 1 and w is wl))
                            last.then_inc(gu, 1)
                    pe.wait_ge(dlr, it + 2)
                    for n in range(ND):
                        i, c = n // 2, n % 2
                        if n % NT == 0:
                            pe.wait_ge(alr, it * UN + (3 + n // NT + 2))
                        pe.wait_ge(add, it * ND + (n + 1))
                        for m in range(MC):
                            for x, w in ((ah, dh), (ah, dl), (al, dh)):
                                last = pe.matmul(ps_d[:, n % 4], x[:, m, P * i:P * i + P], w[:, m, half(c)],
                                                 start=(m == 0 and x is ah and w is dh), stop=(m == MC - 1 and x is al))
                        last.then_inc(dm, 1)

            @block.vector
            def _(dve):
                dve.sem_inc(gat, 2)
                dve.sem_inc(alr, 2)
                dve.sem_inc(add, 4)
                for n in range(2 * KD):
                    h, t = n // KD, n % KD
                    dve.wait_ge(hfr, n + 1)
                    dve.tensor_copy(hh[:, t, half(h)], sg[:, n % 2]).then_inc(hir, 1)
                    dve.wait_ge(hir, n + 1)
                    dve.tensor_tensor(hl[:, t, half(h)], sg[:, n % 2], hh[:, t, half(h)].bitcast(F32),
                                      ALU.subtract).then_inc(lor, 1)
                dve.wait_ge(g2_loaded, 16)

                def units(it):
                    dve.wait_ge(dr_loaded, it * 16 + 16)
                    for m in range(MC):
                        ins = dve.tensor_tensor(dr[:, m], dr[:, m], g2[:], ALU.mult)
                    ins.then_inc(dsc, 1)
                    for u in range(UN):
                        m, h = u // 2, u % 2
                        dve.wait_ge(sil, it * UN + (u + 1))
                        dve.wait_ge(alr, it * UN + (u + 1))
                        dve.tensor_tensor(af[:, u % 2], sg[:, u % 2], ps_u[:, u % 2], ALU.mult).then_inc(gat, 1)
                        dve.wait_ge(gat, it * UN + (u + 1 + 2))
                        dve.wait_ge(dm, it * ND + (NT * h + NT))
                        dve.tensor_copy(ah[:, m, half(h)], af[:, u % 2]).then_inc(ahr, 1)
                        dve.wait_ge(ahr, it * UN + (u + 1))
                        dve.tensor_tensor(al[:, m, half(h)], af[:, u % 2], ah[:, m, half(h)].bitcast(F32),
                                          ALU.subtract).then_inc(alr, 1)

                def add_down(it, n):
                    i, c = n // 2, n % 2
                    dve.wait_ge(dm, it * ND + (n + 1 + ND))
                    dve.wait_ge(add, it * ND + (n + 1))
                    dve.tensor_tensor(g.x1[:, i, half(c)], ps_d[:, n % 4], g.x1[:, i, half(c)], ALU.add).then_inc(add, 1)

                def final(i):
                    dve.wait_ge(rfr, i + 1)
                    dve.scalar_tensor_tensor(out=g.x1[:, i], in0=g.x1[:, i], scalar=rf[:, i:i + 1], in1=afin,
                                             op0=ALU.mult, op1=ALU.mult).then_inc(om, 1)
                    if i % 2 == 0:
                        dve.wait_ge(om, i + 1)
                        dve.tensor_tensor(g.x1[:, i], g.x1[:, i], bfin, ALU.add).then_inc(od, 1)

                with dve.Fori(0, NCH - 1) as it:
                    units(it)
                    for n in range(ND):
                        add_down(it, n)
                units(NCH - 1)
                dve.wait_ge(ab_loaded, 32)
                LAG = 2
                for i in range(NT + LAG):
                    if i < NT:
                        for c in range(2):
                            add_down(NCH - 1, 2 * i + c)
                    if i >= LAG:
                        final(i - LAG)


class Names:
    pass


def emit(nc, A, out, upto=9):
    with ExitStack() as ctx:
        k = Kit(nc)
        scr = nc.dram_tensor("scr_qkv", [16, 2, P, SEQ], F32, kind="Internal").ap()
        vecs = nc.dram_tensor("scr_vectors", [4, D], F32, kind="Internal").ap()
        g = Names()
        g.ident = sbuf(nc, ctx, "ident", [P, P])
        g.ones = sbuf(nc, ctx, "ones", [P, P])
        g.nhalf = sbuf(nc, ctx, "nhalf", [P, NT])
        g.cols = sbuf(nc, ctx, "cols", [P, P])
        g.csil = sbuf(nc, ctx, "csil", [P, KD])
        g.a2 = sbuf(nc, ctx, "a2", [P, KD])
        g.b2 = sbuf(nc, ctx, "b2", [P, KD])
        g.ss2 = sbuf(nc, ctx, "ss2", [P, NT])
        with ExitStack() as co:
            with ExitStack() as c03:
                g.bigid = sbuf(nc, c03, "big_ident", [P, P], F32R)
                g.tneg_f = sbuf(nc, c03, "tneg_f", [P, P])
                g.tneg = sbuf(nc, c03, "tneg", [P, P], F32R)
                g.nneg = sbuf(nc, c03, "nneg", [P, P], F32R)
                g.qscale = sbuf(nc, c03, "qscale", [P, 16])
                g.nslope = sbuf(nc, c03, "nslope", [P, NH])
                g.a1 = sbuf(nc, c03, "a1", [P, KD])
                g.b1 = sbuf(nc, c03, "b1", [P, KD])
                g.wtok = sbuf(nc, c03, "wtok", [P, NT, NIH])
                g.rkv = sbuf(nc, c03, "rkv", [P, NT])
                g.dist = sbuf(nc, c03, "dist", [P, SEQ])
                g.score = sbuf(nc, c03, "score", [P, soff(NT)])
                g.kdh = sbuf(nc, c03, "kdh", [P, SEQ], F32R)
                g.kdl = sbuf(nc, c03, "kdl", [P, SEQ], F32R)
                g.vd = sbuf(nc, c03, "vd", [P, NT, P], F32R)
                with ExitStack() as c01:
                    g.hTh = sbuf(nc, c01, "hTh", [P, KD, SEQ], F32R)
                    g.hTl = sbuf(nc, c01, "hTl", [P, KD, SEQ], F32R)
                    with ExitStack() as c0:
                        g.dist_i = sbuf(nc, c0, "dist_i", [P, SEQ], I32)
                        phase0(nc, k, g, A)
                    if upto >= 1:
                        phase1(nc, k, g, A, scr)
                k.release()
                g.osb = co.enter_context(nc.sbuf_tensor("o_sbT", [P, NPAIR, SEQ], F32, side="right"))
                g.otok = co.enter_context(nc.sbuf_tensor("o_dtok", [P, NT, NH * HD], F32, side="right"))
                if upto >= 2:
                    phase2(nc, k, g, scr)
                if upto >= 3:
                    phase3(nc, k, g, A, scr, vecs)
            k.release()
            g.x1 = sbuf(nc, ctx, "x1", [P, NT, D])
            if upto >= 4:
                phase4(nc, k, g, A, vecs)
        if upto >= 5:
            phase5(nc, k, g, A, vecs, out)
        k.release()


_INS = ["x", "c", "w_mod", "b_mod", "norm1_gain", "norm2_gain", "w_in", "kv_gain", "w_uk", "w_uv", "sb_out_gain",
        "dsa_out_gain", "w_o", "w_gate", "w_up", "w_down", "w_mod_final", "b_mod_final", "final_gain"]
_OUTS = [((1, SEQ, D), "float32")]


def kernel(**inputs):
    import numpy as _np
    import concourse.bacc as _bacc
    from concourse import mybir as _mybir
    from concourse.bass_utils import run_bass_kernel_spmd as _run

    nc = _bacc.Bacc("TRN2", target_bir_lowering=False, num_devices=1)
    arrays, args = {}, {}
    for name in _INS:
        a = _np.ascontiguousarray(inputs[name])
        arrays[f"in_{name}_dram"] = a
        args[name] = nc.dram_tensor(f"in_{name}_dram", a.shape, _mybir.dt.from_np(a.dtype), kind="ExternalInput").ap()
    out = nc.dram_tensor("out_0_dram", _OUTS[0][0], _mybir.dt.float32, kind="ExternalOutput").ap()
    emit(nc, args, out)
    r = _run(nc, [arrays], core_ids=[0])
    return r.results[0]["out_0_dram"]
```
